# Optimizing a Trainium2 kernel written in Bass

```python
import math
import jax, jax.numpy as jnp
from jax import lax
import numpy as np

D_MODEL = 1024
BATCH = 1
SEQ = 512
DEPTH = 1

CHUNK = 64
N_META = 16
BLOCK = 128
N_MIXERS = 3

POOL_WINDOWS = (2, 4, 8, 16)
N_POOL_GROUPS = len(POOL_WINDOWS)
POOL_GROUP = D_MODEL // N_POOL_GROUPS

SWA_HEAD_DIM = 64
SWA_Q_HEADS = D_MODEL // SWA_HEAD_DIM
SWA_KV_HEADS = 2
SWA_WINDOW = 128
SWA_WINDOW_CHUNKS = SWA_WINDOW // CHUNK

DIFF_HEAD_DIM = 64
DIFF_HEADS = D_MODEL // (2 * DIFF_HEAD_DIM)
DIFF_EPS = 1e-5

N_EXPERTS = 32
TOP_K = 4
D_EXPERT = D_MODEL
SWIGLU_ALPHA = 1.702
SWIGLU_LIMIT = 7.0
MOE_BLOCK = 128

DEEPNORM_ALPHA = (2 * DEPTH) ** 0.25
DEEPNORM_BETA = (8 * DEPTH) ** -0.25
LN_EPS = 1e-5

N_POOL_LAYERS = len(range(0, DEPTH, N_MIXERS))
N_SWA_LAYERS = len(range(1, DEPTH, N_MIXERS))
N_DIFF_LAYERS = len(range(2, DEPTH, N_MIXERS))

kernel_name = "hybrid_pool_swa_diff_moe_trunk"

F32 = jnp.float32

def _layer_norm(x, g, b):
    xf = x.astype(F32)
    mu = xf.mean(-1, keepdims=True)
    var = jnp.mean(jnp.square(xf - mu), -1, keepdims=True)
    return ((xf - mu) * lax.rsqrt(var + LN_EPS) * g.astype(F32) + b.astype(F32)).astype(x.dtype)

def _sink_softmax(scores, sink):
    m = jnp.maximum(scores.max(-1, keepdims=True), sink)
    p = jnp.exp(scores - m)
    return p / (p.sum(-1, keepdims=True) + jnp.exp(sink - m))

def _pool_mixer(x, w, scale):
    b, l, d = x.shape
    xf = x.astype(F32)
    cs = jnp.concatenate([jnp.zeros((b, 1, d), F32), jnp.cumsum(xf, axis=1)], axis=1)
    outs = []
    for g, win in enumerate(POOL_WINDOWS):
        c = slice(g * POOL_GROUP, (g + 1) * POOL_GROUP)
        csg = cs[:, :, c]
        lagged = jnp.concatenate([jnp.zeros((b, win - 1, POOL_GROUP), F32), csg[:, :l - win + 1]], axis=1)
        count = jnp.minimum(jnp.arange(1, l + 1), win).astype(F32)
        outs.append((csg[:, 1:] - lagged) / count[None, :, None] - xf[:, :, c])
    pooled = jnp.stack(outs, axis=2).astype(x.dtype)
    y = jnp.einsum('blgc,gce->blge', pooled, w).reshape(b, l, d)
    return y * scale

def _swa_mixer(x, wqkv, bqkv, wo, bo, sinks):
    b, l, _ = x.shape
    s = l - N_META
    nb = s // BLOCK
    hq, hkv, dh = SWA_Q_HEADS, SWA_KV_HEADS, SWA_HEAD_DIM
    grp = hq // hkv
    qkv = jnp.einsum('bld,de->ble', x, wqkv) + bqkv
    q = qkv[..., :hq * dh].reshape(b, l, hkv, grp, dh) * (dh ** -0.5)
    k = qkv[..., hq * dh:(hq + hkv) * dh].reshape(b, l, hkv, dh)
    v = qkv[..., (hq + hkv) * dh:].reshape(b, l, hkv, dh)
    sink = sinks.astype(F32).reshape(hkv, grp)
    qm, km, vm = q[:, :N_META], k[:, :N_META], v[:, :N_META]
    s_mm = jnp.einsum('bikgd,bmkd->bkgim', qm, km, preferred_element_type=F32)
    p_mm = _sink_softmax(s_mm, sink[None, :, :, None, None]).astype(v.dtype)
    o_meta = jnp.einsum('bkgim,bmkd->bikgd', p_mm, vm)
    qr = q[:, N_META:].reshape(b, nb, BLOCK, hkv, grp, dh)

    def _band(t):
        tp = jnp.pad(t[:, N_META:], ((0, 0), (BLOCK, 0), (0, 0), (0, 0))).reshape(b, nb + 1, BLOCK, hkv, dh)
        return jnp.concatenate([tp[:, :-1], tp[:, 1:]], axis=2)

    kb, vb = _band(k), _band(v)
    q_idx = jnp.arange(nb)[:, None] * BLOCK + jnp.arange(BLOCK)[None]
    k_idx = jnp.arange(nb)[:, None] * BLOCK - BLOCK + jnp.arange(2 * BLOCK)[None]
    qc = (q_idx // CHUNK)[:, :, None]
    kc = (k_idx // CHUNK)[:, None, :]
    valid = (k_idx[:, None, :] >= 0) & (kc <= qc) & (kc > qc - SWA_WINDOW_CHUNKS)
    s_band = jnp.einsum('bjikgd,bjrkd->bkgjir', qr, kb, preferred_element_type=F32)
    s_band = jnp.where(valid, s_band, -jnp.inf)
    s_meta = jnp.einsum('bjikgd,bmkd->bkgjim', qr, km, preferred_element_type=F32)
    p = _sink_softmax(jnp.concatenate([s_meta, s_band], axis=-1),
                      sink[None, :, :, None, None, None]).astype(v.dtype)
    o_real = (jnp.einsum('bkgjim,bmkd->bjikgd', p[..., :N_META], vm)
              + jnp.einsum('bkgjir,bjrkd->bjikgd', p[..., N_META:], vb))
    o = jnp.concatenate([o_meta.reshape(b, N_META, hq * dh), o_real.reshape(b, s, hq * dh)], axis=1)
    return jnp.einsum('ble,ed->bld', o, wo) + bo

def _lambda_init(layer_idx):
    return 0.8 - 0.6 * math.exp(-0.3 * layer_idx)

def _diff_mixer(x, wqkv, wo, lam, subln_g, lambda_init):
    b, l, d = x.shape
    s = l - N_META
    nb = s // BLOCK
    h, dh = DIFF_HEADS, DIFF_HEAD_DIM
    qkv = jnp.einsum('bld,de->ble', x, wqkv)
    q = qkv[..., :d].reshape(b, l, h, 2, dh) * (dh ** -0.5)
    k = qkv[..., d:2 * d].reshape(b, l, h, 2, dh)
    v = qkv[..., 2 * d:].reshape(b, l, h, 2 * dh)
    lam_f = lam.astype(F32)
    lmbda = jnp.exp(jnp.sum(lam_f[0] * lam_f[1])) - jnp.exp(jnp.sum(lam_f[2] * lam_f[3])) + lambda_init
    s_mm = jnp.einsum('bihtd,bnhtd->bhtin', q[:, :N_META], k[:, :N_META], preferred_element_type=F32)
    p_mm = jax.nn.softmax(s_mm, axis=-1)
    a_mm = (p_mm[:, :, 0] - lmbda * p_mm[:, :, 1]).astype(v.dtype)
    o_meta = jnp.einsum('bhin,bnhe->bihe', a_mm, v[:, :N_META])
    k_real = jnp.arange(l) - N_META
    kc = jnp.where(k_real < 0, -1, k_real // CHUNK)
    q_blocks = jnp.moveaxis(q[:, N_META:].reshape(b, nb, BLOCK, h, 2, dh), 1, 0)

    def _block(args):
        j, qb = args
        qc = (j * BLOCK + jnp.arange(BLOCK)) // CHUNK
        valid = kc[None, :] <= qc[:, None]
        sc = jnp.einsum('bihtd,bnhtd->bhtin', qb, k, preferred_element_type=F32)
        p = jax.nn.softmax(jnp.where(valid, sc, -jnp.inf), axis=-1)
        a = (p[:, :, 0] - lmbda * p[:, :, 1]).astype(v.dtype)
        return jnp.einsum('bhin,bnhe->bihe', a, v)

    o_real = lax.map(_block, (jnp.arange(nb), q_blocks))
    o_real = jnp.moveaxis(o_real, 0, 1).reshape(b, s, h, 2 * dh)
    o = jnp.concatenate([o_meta, o_real], axis=1).astype(F32)
    o = o * lax.rsqrt(jnp.mean(jnp.square(o), -1, keepdims=True) + DIFF_EPS) * subln_g.astype(F32)
    o = (o * (1.0 - lambda_init)).astype(x.dtype).reshape(b, l, d)
    return jnp.einsum('ble,ed->bld', o, wo)

def _moe(x, router_w, router_b, wgu, bgu, wd, bd):
    b, l, d = x.shape
    t = b * l
    xt = x.reshape(t, d)
    logits = (jnp.einsum('td,ed->te', xt, router_w, preferred_element_type=F32) + router_b.astype(F32))
    top_v, top_e = lax.top_k(logits, TOP_K)
    gates = jax.nn.softmax(top_v, axis=-1)
    n_asg = t * TOP_K
    flat_e = top_e.reshape(-1)
    order = jnp.argsort(flat_e)
    sorted_e = flat_e[order]
    sorted_tok = (order // TOP_K).astype(jnp.int32)
    sorted_gate = gates.reshape(-1)[order]
    counts = jnp.bincount(flat_e, length=N_EXPERTS)
    starts = jnp.cumsum(counts) - counts
    padded = (counts + MOE_BLOCK - 1) // MOE_BLOCK * MOE_BLOCK
    pends = jnp.cumsum(padded)
    pstarts = pends - padded
    dest = pstarts[sorted_e] + (jnp.arange(n_asg) - starts[sorted_e])
    n_blocks = -(-n_asg // MOE_BLOCK) + N_EXPERTS
    n_rows = n_blocks * MOE_BLOCK
    row_tok = jnp.full((n_rows,), t, jnp.int32).at[dest].set(sorted_tok)
    row_gate = jnp.zeros((n_rows,), F32).at[dest].set(sorted_gate)
    block_e = jnp.minimum(jnp.searchsorted(pends, jnp.arange(n_blocks) * MOE_BLOCK, side='right'),
                          N_EXPERTS - 1)
    x_pad = jnp.concatenate([xt, jnp.zeros((1, d), xt.dtype)], axis=0)
    row_x = x_pad[row_tok].reshape(n_blocks, MOE_BLOCK, d)

    def _expert_block(args):
        xb, e = args
        gu = xb @ wgu[e] + bgu[e]
        gate = jnp.minimum(gu[:, :D_EXPERT], SWIGLU_LIMIT)
        up = jnp.clip(gu[:, D_EXPERT:], -SWIGLU_LIMIT, SWIGLU_LIMIT)
        hdn = (up + 1.0) * gate * jax.nn.sigmoid(gate * SWIGLU_ALPHA)
        return hdn @ wd[e] + bd[e]

    ys = lax.map(_expert_block, (row_x, block_e)).reshape(n_rows, d)
    ys = ys * row_gate[:, None].astype(ys.dtype)
    out = jax.ops.segment_sum(ys, row_tok, num_segments=t + 1)[:t]
    return out.reshape(b, l, d)

def _nrm(k, shape, std):
    return jax.random.normal(k, shape, F32) * std

def setup_inputs(seed: int = 0) -> dict:
    key = jax.random.key(seed)
    ks = iter(jax.random.split(key, 32))
    d, dh_s, dh_d = D_MODEL, SWA_HEAD_DIM, DIFF_HEAD_DIM
    x = _nrm(next(ks), (BATCH, SEQ, d), 1.0)
    meta_tokens = _nrm(next(ks), (N_META, d), 1.0)
    pool_w = _nrm(next(ks), (N_POOL_LAYERS, N_POOL_GROUPS, POOL_GROUP, POOL_GROUP),
                  POOL_GROUP ** -0.5 * DEEPNORM_BETA)
    pool_scale = 1.0 + _nrm(next(ks), (N_POOL_LAYERS, d), 0.02)
    swa_qk = _nrm(next(ks), (N_SWA_LAYERS, d, (SWA_Q_HEADS + SWA_KV_HEADS) * dh_s), d ** -0.5)
    swa_v = _nrm(next(ks), (N_SWA_LAYERS, d, SWA_KV_HEADS * dh_s), d ** -0.5 * DEEPNORM_BETA)
    swa_wqkv = jnp.concatenate([swa_qk, swa_v], axis=-1)
    swa_bqkv = _nrm(next(ks), (N_SWA_LAYERS, (SWA_Q_HEADS + 2 * SWA_KV_HEADS) * dh_s), 0.02)
    swa_wo = _nrm(next(ks), (N_SWA_LAYERS, SWA_Q_HEADS * dh_s, d), (SWA_Q_HEADS * dh_s) ** -0.5 * DEEPNORM_BETA)
    swa_bo = _nrm(next(ks), (N_SWA_LAYERS, d), 0.02)
    swa_sinks = _nrm(next(ks), (N_SWA_LAYERS, SWA_Q_HEADS), 0.5)
    diff_qk = _nrm(next(ks), (N_DIFF_LAYERS, d, 2 * d), d ** -0.5)
    diff_v = _nrm(next(ks), (N_DIFF_LAYERS, d, d), d ** -0.5 * DEEPNORM_BETA)
    diff_wqkv = jnp.concatenate([diff_qk, diff_v], axis=-1)
    diff_wo = _nrm(next(ks), (N_DIFF_LAYERS, d, d), d ** -0.5 * DEEPNORM_BETA)
    diff_lambda = _nrm(next(ks), (N_DIFF_LAYERS, 4, dh_d), 0.1)
    diff_subln_g = 1.0 + _nrm(next(ks), (N_DIFF_LAYERS, 2 * dh_d), 0.02)
    router_w = _nrm(next(ks), (DEPTH, N_EXPERTS, d), d ** -0.5)
    router_b = _nrm(next(ks), (DEPTH, N_EXPERTS), 0.01)
    moe_wgu = _nrm(next(ks), (DEPTH, N_EXPERTS, d, 2 * D_EXPERT), d ** -0.5)
    moe_bgu = _nrm(next(ks), (DEPTH, N_EXPERTS, 2 * D_EXPERT), 0.02)
    moe_wd = _nrm(next(ks), (DEPTH, N_EXPERTS, D_EXPERT, d), D_EXPERT ** -0.5 * DEEPNORM_BETA)
    moe_bd = _nrm(next(ks), (DEPTH, N_EXPERTS, d), 0.02)
    ln_g = 1.0 + _nrm(next(ks), (DEPTH, 2, d), 0.02)
    ln_b = _nrm(next(ks), (DEPTH, 2, d), 0.02)
    return {"x": x, "meta_tokens": meta_tokens, "pool_w": pool_w, "pool_scale": pool_scale,
            "swa_wqkv": swa_wqkv, "swa_bqkv": swa_bqkv, "swa_wo": swa_wo, "swa_bo": swa_bo,
            "swa_sinks": swa_sinks, "diff_wqkv": diff_wqkv, "diff_wo": diff_wo,
            "diff_lambda": diff_lambda, "diff_subln_g": diff_subln_g, "router_w": router_w,
            "router_b": router_b, "moe_wgu": moe_wgu, "moe_bgu": moe_bgu, "moe_wd": moe_wd,
            "moe_bd": moe_bd, "ln_g": ln_g, "ln_b": ln_b}

def reference(x, meta_tokens, pool_w, pool_scale, swa_wqkv, swa_bqkv, swa_wo, swa_bo, swa_sinks,
              diff_wqkv, diff_wo, diff_lambda, diff_subln_g, router_w, router_b, moe_wgu, moe_bgu,
              moe_wd, moe_bd, ln_g, ln_b):
    b = x.shape[0]
    meta = jnp.broadcast_to(meta_tokens[None].astype(x.dtype), (b, N_META, D_MODEL))
    h = jnp.concatenate([meta, x], axis=1)
    for i in range(DEPTH):
        kind, slot = i % N_MIXERS, i // N_MIXERS
        if kind == 0:
            y = _pool_mixer(h, pool_w[slot], pool_scale[slot])
        elif kind == 1:
            y = _swa_mixer(h, swa_wqkv[slot], swa_bqkv[slot], swa_wo[slot], swa_bo[slot], swa_sinks[slot])
        else:
            y = _diff_mixer(h, diff_wqkv[slot], diff_wo[slot], diff_lambda[slot], diff_subln_g[slot],
                            _lambda_init(i))
        h = _layer_norm(DEEPNORM_ALPHA * h + y, ln_g[i, 0], ln_b[i, 0])
        y = _moe(h, router_w[i], router_b[i], moe_wgu[i], moe_bgu[i], moe_wd[i], moe_bd[i])
        h = _layer_norm(DEEPNORM_ALPHA * h + y, ln_g[i, 1], ln_b[i, 1])
    return h[:, N_META:]


_drawn_inputs = setup_inputs


def setup_inputs(seed=0):
    import zlib

    import numpy as np

    out = dict(_drawn_inputs(seed))
    spreads = {}
    factors = {'meta_tokens': 4.289,
     'pool_scale': 3.631,
     'router_b': 2.972,
     'moe_bgu': 8.0,
     'moe_bd': 6.429}
    for name, (base, spread) in spreads.items():
        noise = np.random.default_rng([zlib.crc32(name.encode()), seed]).standard_normal(out[name].shape)
        drawn = base * np.exp(spread * noise) if base else spread * noise
        out[name] = __import__('jax').numpy.asarray(drawn.astype(out[name].dtype))
    for name, factor in factors.items():
        out[name] = (out[name] * factor).astype(out[name].dtype)
    return out
```

```python
from contextlib import ExitStack

import numpy as np

import concourse.bass as bass
from concourse import mybir

P = 128
SEQ, D, META = 512, 1024, 16
NT = SEQ // P
KD = D // P
WINDOWS = (2, 4, 8, 16)
NG = len(WINDOWS)
GW = D // NG
E, TOPK, F = 32, 4, 1024
BANK = 512
NB = 3
ALPHA = 2.0 ** 0.25
LN_EPS = 1e-5
LIMIT, SWISH = 7.0, 1.702
EP = E + 1
BQ = 2 * F // 4
ABSENT = 4096
MORE = SEQ // P - 1
NX = MORE * E

F32, BF16, I32, U32 = mybir.dt.float32, mybir.dt.bfloat16, mybir.dt.int32, mybir.dt.uint32
ALU, ACT, AX = mybir.AluOpType, mybir.ActivationFunctionType, mybir.AxisListType

C_ID, C_BAND = 0, P
C_SLOT = C_BAND + NG * 2 * P
C_EXP = C_SLOT + P
C_TRI = C_EXP + E
C_ONE3 = C_TRI + P
C_TOK = C_ONE3 + P
C_SPARE = C_TOK + NT
C_ALL = C_SPARE + 1


def shape_constants():
    c = np.zeros((P, C_ALL), np.float32)
    i = np.arange(P)
    c[:, C_ID:C_ID + P] = np.eye(P)
    s, t = i[:, None], i[None, :]
    for g, win in enumerate(WINDOWS):
        own = ((s <= t) & (s > t - win)) / win - (s == t)
        before = (s - P > t - win) / win
        at = C_BAND + g * 2 * P
        c[:, at:at + P], c[:, at + P:at + 2 * P] = own, before
    c[:, C_SLOT:C_SLOT + P] = i + 1
    c[:, C_EXP:C_EXP + E] = np.arange(E)
    c[:, C_TRI:C_TRI + P] = s < t
    c[:NB, C_ONE3:C_ONE3 + P] = 1
    c[:, C_TOK:C_TOK + NT] = i[:, None] + P * np.arange(NT) - ABSENT
    c[:, C_SPARE] = SEQ + i
    return c


def trunk(nc, x, meta, consts, pool_w, pool_scale, router_wt, router_b, wgu, bgu, wd, bd, ln_g, ln_b, out):
    ctx = ExitStack()
    with ctx:
        def sb(name, shape, dt=F32):
            return ctx.enter_context(nc.sbuf_tensor(name, shape, dt))

        def sem(name):
            return ctx.enter_context(nc.semaphore(name))

        h1_dram = nc.dram_tensor("h1_rows", [SEQ, D], F32, kind="Internal").ap()
        acc_dram = nc.dram_tensor("acc_rows", [SEQ + P, D], F32, kind="Internal").ap()
        gub_dram = nc.dram_tensor("gu_bias_parts", [NB, E, 2 * F], BF16, kind="Internal").ap()
        db_dram = nc.dram_tensor("d_bias_parts", [NB, E, D], BF16, kind="Internal").ap()

        cst = sb("cst", [P, C_ALL])
        gu_ring = sb("gu_ring", [P, KD, 2 * F])
        wd_ring = sb("wd_ring", [P, KD, D])
        xin = sb("xin", [P, NT, D])
        prev = sb("prev", [P, D])
        turned = sb("turned", [P, 2, KD, P])
        pw = sb("pw", [P, NG * 2, GW])
        z = sb("z", [P, NT, D])
        h1 = sb("h1", [P, NT, D])
        wide = sb("wide", [P, 3, D])
        rwt = sb("rwt", [P, KD, E])
        rb = sb("rb", [P, E])
        stats = sb("stats", [P, NT, 2, 6])
        mv = sb("mv", [P, NT, 2])
        var = sb("var", [P, NT])
        std = sb("std", [P, NT])
        rstd = sb("rstd", [P, NT])
        fix = sb("fix", [P, NT])
        brow = z[:, 2, 0:BQ + D // 4]
        bres = z[:, 3, 0:BQ + D // 4]
        bpart = sb("bpart", [P, NB, BQ + D // 4], BF16)
        logit = sb("logit", [P, NT, E])
        top = sb("top", [P, NT, 8])
        topi = sb("topi", [P, NT, 8], U32)
        topf = sb("topf", [P, NT, 8])
        gexp = sb("gexp", [P, NT, TOPK])
        gsum = sb("gsum", [P, NT])
        gates = sb("gates", [P, NT, TOPK])
        pick = xin[:, 0, 0:NT * TOPK * E].rearrange("p (t k e) -> p t k e", t=NT, k=TOPK)
        pickg = xin[:, 1, 0:NT * TOPK * E].rearrange("p (t k e) -> p t k e", t=NT, k=TOPK)
        chosen = sb("chosen", [P, NT, E])
        chosen16 = sb("chosen16", [P, NT, E], BF16)
        place = sb("place", [P, NT, EP])
        value = sb("value", [P, NT, EP, 2])
        tri16 = sb("tri16", [P, P], BF16)
        ones16 = sb("ones16", [P, P], BF16)
        three16 = sb("three16", [P, P], BF16)
        count = sb("count", [1, E])
        most = sb("most", [1, 1], I32)
        hot = xin[:, 3, 0:NT * P].rearrange("p (t s) -> p t s", t=NT)
        val = sb("val", [P, NT, 2])
        slot = sb("slot", [P, EP, 2])
        gidx = sb("gidx", [P, 1], I32)
        sidx_all = sb("sidx_all", [P, EP], I32)
        sidx = sb("sidx", [P, 1], I32)
        xg = h1[:, 0, :]
        xt = h1[:, 2, :].rearrange("p (k n) -> p k n", n=P)
        gate = z[:, 0, :]
        sig = z[:, 1, :]
        up = z[:, 2, :]
        hid = z[:, 3, :]
        ht = h1[:, 3, :].rearrange("p (k n) -> p k n", n=P)
        y = h1[:, 1, :]
        gu_bias = sb("gu_bias", [P, 2 * F], BF16)
        d_bias = sb("d_bias", [P, D], BF16)
        place_x = xin[:, 2, 0:NT * NX].rearrange("p (t n) -> p t n", t=NT)
        over = sb("over", [1, NX])
        seq_f = sb("seq_f", [1, NX])
        over_i = sb("over_i", [1, NX], I32)
        seq_i = sb("seq_i", [1, NX], I32)
        slot_x = sb("slot_x", [P, 2])

        ident = cst[:, C_ID:C_ID + P]

        ps_gu = ctx.enter_context(nc.psum_tensor("ps_gu", [P, 4, BANK], F32))
        ps_y = ctx.enter_context(nc.psum_tensor("ps_y", [P, 2, BANK], F32))
        ps_t = ctx.enter_context(nc.psum_tensor("ps_t", [P, 2, BANK], F32))

        x_landed = [sem(f"x_landed{t}") for t in range(NT)]
        consts_landed = sem("consts_landed")
        meta_cleared = sem("meta_cleared")
        meta_landed = sem("meta_landed")
        pw_landed = sem("pw_landed")
        wide_landed = sem("wide_landed")
        router_landed = sem("router_landed")
        biases_landed = sem("biases_landed")
        pooled = sem("pooled")
        pooled_copied = sem("pooled_copied")
        mixed = sem("mixed")
        mix_evacuated = sem("mix_evacuated")
        ln_step = sem("ln_step")
        stats_ready = sem("stats_ready")
        var_ready = sem("var_ready")
        std_ready = sem("std_ready")
        rstd_step = sem("rstd_step")
        normed = sem("normed")
        gained = sem("gained")
        h1_ready = sem("h1_ready")
        h1_scaled = sem("h1_scaled")
        h1_stored = sem("h1_stored")
        acc_stored = sem("acc_stored")
        h1_turned = sem("h1_turned")
        h1_copied = sem("h1_copied")
        logits_done = sem("logits_done")
        logits_read = sem("logits_read")
        bias_step = sem("bias_step")
        bias_stored = sem("bias_stored")
        zeros_set = sem("zeros_set")
        small_cast = sem("small_cast")
        route_step = sem("route_step")
        exp_in = sem("exp_in")
        exp_done = sem("exp_done")
        chosen_ready = sem("chosen_ready")
        ranked = sem("ranked")
        place_ready = sem("place_ready")
        most_ready = sem("most_ready")
        gu_landed = [sem(f"gu_landed{k}") for k in range(KD)]
        gu_used = sem("gu_used")
        wd_landed = [sem(f"wd_landed{k}") for k in range(KD // 2)]
        wd_used = sem("wd_used")
        gub_landed = sem("gub_landed")
        gub_used = sem("gub_used")
        db_landed = sem("db_landed")
        db_used = sem("db_used")
        hot_step = sem("hot_step")
        hot_used = sem("hot_used")
        gidx_ready = sem("gidx_ready")
        xg_landed = sem("xg_landed")
        xg_turned = sem("xg_turned")
        xt_ready = sem("xt_ready")
        act_step = sem("act_step")
        gate_ready = sem("gate_ready")
        up_ready = sem("up_ready")
        y_free = sem("y_free")
        sig_ready = sem("sig_ready")
        hid_ready = sem("hid_ready")
        hid_turned = sem("hid_turned")
        ht_ready = sem("ht_ready")
        y_ready = sem("y_ready")
        sidx_ready = sem("sidx_ready")
        rows_added = sem("rows_added")
        x_tables = sem("x_tables")
        x_step = sem("x_step")
        x_free = sem("x_free")
        x_weights = sem("x_weights")
        x_hot = sem("x_hot")
        x_listed = sem("x_listed")
        x_gidx = sem("x_gidx")
        x_rows = sem("x_rows")
        x_turned = sem("x_turned")
        x_xt = sem("x_xt")
        x_gu = sem("x_gu")
        x_gate = sem("x_gate")
        x_up = sem("x_up")
        x_upgate = sem("x_upgate")
        x_sig = sem("x_sig")
        x_hid = sem("x_hid")
        x_hturned = sem("x_hturned")
        x_ht = sem("x_ht")
        x_d = sem("x_d")
        x_y = sem("x_y")
        x_added = sem("x_added")
        x_end = sem("x_end")
        wide2_landed = sem("wide2_landed")
        sums_landed = [sem(f"sums_landed{t}") for t in range(NT)]
        last_step = sem("last_step")
        last_stats = sem("last_stats")
        last_var = sem("last_var")
        last_std = sem("last_std")
        last_rstd = sem("last_rstd")
        last_normed = sem("last_normed")
        last_gained = sem("last_gained")
        last_ready = sem("last_ready")
        out_stored = sem("out_stored")

        wgu_v = wgu.rearrange("e (k p) n -> e p k n", p=P)
        wd_v = wd.rearrange("e (k p) n -> e p k n", p=P)

        def turn(dst, src):
            for k in range(KD):
                last = nc.tensor.transpose(dst[:, k // 4, (k % 4) * P:(k % 4 + 1) * P],
                                           src[:, k * P:(k + 1) * P], ident)
            return last

        def gate_up_bias():
            for n in range(4):
                last = nc.tensor.matmul(ps_gu[:, n, :], three16[:], gu_bias[:, n * BANK:(n + 1) * BANK],
                                        start=True, stop=False)
            return last

        def gate_up(k):
            for n in range(4):
                last = nc.tensor.matmul(ps_gu[:, n, :], xt[:, k, :], gu_ring[:, k, n * BANK:(n + 1) * BANK],
                                        start=False, stop=(k == KD - 1))
            return last

        def down_bias():
            for n in range(2):
                last = nc.tensor.matmul(ps_y[:, n, :], three16[:], d_bias[:, n * BANK:(n + 1) * BANK],
                                        start=True, stop=False)
            return last

        def down(k):
            for n in range(2):
                last = nc.tensor.matmul(ps_y[:, n, :], ht[:, k, :], wd_ring[:, k, n * BANK:(n + 1) * BANK],
                                        start=False, stop=(k == KD - 1))
            return last

        def list_slots(bank):
            for t in range(NT):
                last = nc.tensor.matmul(bank, hot[:, t, :], val[:, t, :], start=(t == 0), stop=(t == NT - 1))
            return last

        block = ctx.enter_context(nc.Block())

        @block.sync
        def _(sp):
            for t in range(NT):
                sp.dma_start(xin[:, t, :], x[0, t * P:(t + 1) * P, :]).then_inc(x_landed[t], 16)
                if t == 0:
                    sp.dma_start(cst[:], consts).then_inc(consts_landed, 16)
            sp.dma_start(pw[:], pool_w[0].rearrange("g (k p) n -> p (g k) n", p=P)).then_inc(pw_landed, 16)

            def load_gu(e, k):
                sp.dma_start(gu_ring[:, k, :], wgu_v[e, :, k, :]).then_inc(gu_landed[k], 16)

            def load_wd(e, k2):
                sp.dma_start(wd_ring[:, 2 * k2:2 * k2 + 2, :], wd_v[e, :, 2 * k2:2 * k2 + 2, :])\
                    .then_inc(wd_landed[k2], 16)

            def load_gu_bias(e):
                sp.dma_start(gu_bias[0:NB, :], gub_dram[:, e, :]).then_inc(gub_landed, 16)

            def load_d_bias(e):
                sp.dma_start(d_bias[0:NB, :], db_dram[:, e, :]).then_inc(db_landed, 16)

            for k in range(KD):
                load_gu(0, k)
            for k2 in range(KD // 2):
                load_wd(0, k2)
            sp.wait_ge(bias_stored, 32 * NB)
            sp.wait_ge(zeros_set, 2)
            load_gu_bias(0)
            load_d_bias(0)
            sp.wait_ge(gub_used, 1)
            load_gu_bias(1)
            for k in range(KD):
                sp.wait_ge(gu_used, k + 1)
                load_gu(1, k)
            with sp.Fori(2, E) as e:
                sp.wait_ge(db_used, e - 1)
                load_d_bias(e - 1)
                for k2 in range(KD // 2):
                    sp.wait_ge(wd_used, (e - 2) * (KD // 2) + (k2 + 1))
                    load_wd(e - 1, k2)
                sp.wait_ge(gub_used, e)
                load_gu_bias(e)
                for k in range(KD):
                    sp.wait_ge(gu_used, (e - 1) * KD + (k + 1))
                    load_gu(e, k)
            sp.wait_ge(db_used, E - 1)
            load_d_bias(E - 1)
            for k2 in range(KD // 2):
                sp.wait_ge(wd_used, (E - 2) * (KD // 2) + k2 + 1)
                load_wd(E - 1, k2)

            sp.wait_ge(most_ready, 1)
            largest = sp.value_load(most[0:1, 0:1], min_val=0, max_val=SEQ)
            with sp.If(largest > P):
                sp.wait_ge(x_tables, 1)
                for j in range(MORE):
                    with sp.Fori(0, E) as e:
                        need = sp.value_load(over_i[0:1, bass.ds(e + j * E, 1)], min_val=0, max_val=1)
                        with sp.If(need > 0):
                            q = sp.value_load(seq_i[0:1, bass.ds(e + j * E, 1)], min_val=1, max_val=NX)
                            sp.wait_ge(x_free, q)
                            sp.dma_start(gu_bias[0:NB, :], gub_dram[:, e, :]).then_inc(x_weights, 16)
                            sp.dma_start(d_bias[0:NB, :], db_dram[:, e, :]).then_inc(x_weights, 16)
                            for k in range(KD):
                                sp.dma_start(gu_ring[:, k, :], wgu_v[e, :, k, :]).then_inc(x_weights, 16)
                            sp.dma_start(wd_ring[:], wd_v[e]).then_inc(x_weights, 16)

            sp.wait_ge(x_end, 1)
            for t in range(NT):
                sp.dma_start(xin[:, t, :], acc_dram[t * P:(t + 1) * P, :]).then_inc(sums_landed[t], 16)
            for t in range(NT):
                sp.wait_ge(last_ready, t + 1)
                sp.dma_start(out[0, t * P:(t + 1) * P, :], h1[:, t, :]).then_inc(out_stored, 16)
            sp.wait_ge(out_stored, 16 * NT)

        @block.scalar
        def _(act):
            act.dma_start(wide[:, 0, :], pool_scale[0].partition_broadcast(P)).then_inc(wide_landed, 16)
            act.wait_ge(meta_cleared, 1)
            act.dma_start(prev[P - META:P, :], meta).then_inc(meta_landed, 16)
            act.dma_start(brow[:, 0:BQ], bgu[0].rearrange("e (q n) -> (e q) n", q=4)).then_inc(biases_landed, 16)
            act.dma_start(brow[:, BQ:], bd[0].rearrange("e (q n) -> (e q) n", q=4)).then_inc(biases_landed, 16)
            act.dma_start(wide[:, 1, :], ln_g[0, 0].partition_broadcast(P)).then_inc(wide_landed, 16)
            act.dma_start(wide[:, 2, :], ln_b[0, 0].partition_broadcast(P)).then_inc(wide_landed, 16)
            act.dma_start(rwt[:], router_wt.rearrange("(k p) e -> p k e", p=P)).then_inc(router_landed, 16)
            act.dma_start(rb[:], router_b[0].partition_broadcast(P)).then_inc(router_landed, 16)

            def copy_turned(dst, src):
                return nc.scalar.activation(dst.rearrange("p (b k) n -> p b (k n)", b=2), src, ACT.Copy)

            def sigmoid():
                return nc.scalar.activation(sig, gate, ACT.Sigmoid, scale=SWISH)

            def weigh(g):
                return nc.scalar.activation(y.rearrange("p (b n) -> p b n", b=2), ps_y[:], ACT.Copy, scale=g)

            for t in range(NT + 2):
                if t < NT:
                    act.wait_ge(pooled, t + 1)
                    if t >= 2:
                        act.wait_ge(mixed, t - 1)
                    copy_turned(turned[:, t % 2], ps_gu[:, 2 * (t % 2):2 * (t % 2) + 2, :])\
                        .then_inc(pooled_copied, 1)
                if t >= 2:
                    act.wait_ge(var_ready, t - 1)
                    nc.scalar.activation(std[:, t - 2:t - 1], var[:, t - 2:t - 1], ACT.Sqrt).then_inc(std_ready, 1)
                if t == 1:
                    act.wait_ge(bias_step, 5)
                    for s in range(NB):
                        act.dma_start(gub_dram[s].rearrange("e (q n) -> (e q) n", q=4), bpart[:, s, 0:BQ])\
                            .then_inc(bias_stored, 16)
                        act.dma_start(db_dram[s].rearrange("e (q n) -> (e q) n", q=4), bpart[:, s, BQ:])\
                            .then_inc(bias_stored, 16)

            for t in range(NT):
                act.wait_ge(h1_ready, t + 1)
                act.dma_start(h1_dram[t * P:(t + 1) * P, :], h1[:, t, :]).then_inc(h1_stored, 16)
                act.wait_ge(h1_turned, t + 1)
                if t >= 2:
                    act.wait_ge(logits_done, t - 1)
                copy_turned(turned[:, t % 2], ps_gu[:, 2 * (t % 2):2 * (t % 2) + 2, :]).then_inc(h1_copied, 1)
                nc.scalar.activation(z[:, t, :], h1[:, t, :], ACT.Copy, scale=ALPHA).then_inc(h1_scaled, 1)
                act.wait_ge(h1_scaled, t + 1)
                act.dma_start(acc_dram[t * P:(t + 1) * P, :], z[:, t, :]).then_inc(acc_stored, 16)
            act.dma_start(acc_dram[SEQ:SEQ + P, :], z[:, 0, :]).then_inc(acc_stored, 16)
            act.dma_start(wide[:, 1, :], ln_g[0, 1].partition_broadcast(P)).then_inc(wide2_landed, 16)
            act.dma_start(wide[:, 2, :], ln_b[0, 1].partition_broadcast(P)).then_inc(wide2_landed, 16)

            act.wait_ge(exp_in, 1)
            nc.scalar.activation(gexp[:], gexp[:], ACT.Exp).then_inc(exp_done, 1)

            act.wait_ge(h1_stored, 16 * NT)
            act.wait_ge(acc_stored, 16 * (NT + 1))
            act.wait_ge(xg_turned, 1)
            copy_turned(xt, ps_t[:]).then_inc(xt_ready, 1)
            act.wait_ge(xg_turned, 2)
            copy_turned(xt, ps_t[:]).then_inc(xt_ready, 1)
            act.wait_ge(gate_ready, 1)
            sigmoid().then_inc(sig_ready, 1)
            act.wait_ge(hid_turned, 1)
            copy_turned(ht, ps_t[:]).then_inc(ht_ready, 1)
            with act.Fori(1, E) as e:
                act.wait_ge(xg_turned, e + 2)
                copy_turned(xt, ps_t[:]).then_inc(xt_ready, 1)
                act.wait_ge(gate_ready, e + 1)
                sigmoid().then_inc(sig_ready, 1)
                act.wait_ge(wd_used, e * (KD // 2))
                act.wait_ge(y_free, e)
                weigh(slot[:, bass.ds(e - 1, 1), 1]).then_inc(y_ready, 1)
                act.wait_ge(hid_turned, e + 1)
                copy_turned(ht, ps_t[:]).then_inc(ht_ready, 1)
            act.wait_ge(wd_used, E * (KD // 2))
            act.wait_ge(y_free, E)
            weigh(slot[:, E - 1, 1:2]).then_inc(y_ready, 1)

            act.wait_ge(most_ready, 1)
            largest = act.value_load(most[0:1, 0:1], min_val=0, max_val=SEQ)
            with act.If(largest > P):
                act.wait_ge(x_tables, 1)
                with act.Fori(0, NX) as n:
                    need = act.value_load(over_i[0:1, bass.ds(n, 1)], min_val=0, max_val=1)
                    with act.If(need > 0):
                        q = act.value_load(seq_i[0:1, bass.ds(n, 1)], min_val=1, max_val=NX)
                        act.wait_ge(x_turned, q)
                        copy_turned(xt, ps_t[:]).then_inc(x_xt, 1)
                        act.wait_ge(x_gate, q)
                        sigmoid().then_inc(x_sig, 1)
                        act.wait_ge(x_hturned, q)
                        copy_turned(ht, ps_t[:]).then_inc(x_ht, 1)
                        act.wait_ge(x_d, q)
                        weigh(slot_x[:, 1:2]).then_inc(x_y, 1)

            for t in range(NT):
                act.wait_ge(last_var, t + 1)
                nc.scalar.activation(std[:, t:t + 1], var[:, t:t + 1], ACT.Sqrt).then_inc(last_std, 1)

        @block.gpsimd
        def _(pool):
            nc.gpsimd.memset(prev[:], 0.0).then_inc(meta_cleared, 1)
            nc.gpsimd.memset(gu_bias[:], 0.0).then_inc(zeros_set, 1)
            nc.gpsimd.memset(d_bias[:], 0.0).then_inc(zeros_set, 1)
            pool.sem_inc(y_free, 1)

            last_row, last_sum = pool.to_reg(SEQ - 1), pool.to_reg(SEQ + P - 1)

            def gather():
                return nc.gpsimd.indirect_dma_start(
                    out=xg, out_offset=None, in_=h1_dram,
                    in_offset=bass.IndirectOffsetOnAxis(ap=gidx[:, 0:1], axis=0),
                    bounds_check=last_row, oob_is_err=False)

            def scatter():
                return nc.gpsimd.indirect_dma_start(
                    out=acc_dram, out_offset=bass.IndirectOffsetOnAxis(ap=sidx[:, 0:1], axis=0),
                    in_=y, in_offset=None,
                    bounds_check=last_sum, oob_is_err=True, compute_op=ALU.add)

            pool.wait_ge(wide_landed, 48)
            for t in range(NT):
                pool.wait_ge(gained, t + 1)
                nc.gpsimd.tensor_tensor(h1[:, t, :], h1[:, t, :], wide[:, 2, :], ALU.add).then_inc(h1_ready, 1)

            pool.wait_ge(h1_stored, 16 * NT)
            pool.wait_ge(h1_scaled, NT)
            pool.wait_ge(gidx_ready, 3)
            gather().then_inc(xg_landed, 16)
            pool.wait_ge(gidx_ready, 6)
            pool.wait_ge(xg_turned, 1)
            gather().then_inc(xg_landed, 16)
            with pool.Fori(1, E) as e:
                listed_e1, turned_e, added_e = pool.to_reg(e * 3 + 6), pool.to_reg(e + 1), pool.to_reg(e * 16)
                pool.wait_ge(h1_stored, 16 * NT)
                pool.wait_ge(gidx_ready, listed_e1)
                pool.wait_ge(xg_turned, turned_e)
                gather().then_inc(xg_landed, 16)
                nc.gpsimd.tensor_copy(sidx[:], sidx_all[:, bass.ds(e - 1, 1)]).then_inc(sidx_ready, 1)
                pool.wait_ge(acc_stored, 16 * (NT + 1))
                pool.wait_ge(sidx_ready, e)
                pool.wait_ge(y_ready, e)
                scatter().then_inc(rows_added, 16)
                pool.wait_ge(rows_added, added_e)
                pool.sem_inc(y_free, 1)
            nc.gpsimd.tensor_copy(sidx[:], sidx_all[:, E - 1:E]).then_inc(sidx_ready, 1)
            pool.wait_ge(sidx_ready, E)
            pool.wait_ge(y_ready, E)
            scatter().then_inc(rows_added, 16)
            pool.wait_ge(rows_added, E * 16)
            pool.wait_ge(xg_landed, (E + 1) * 16)

            pool.wait_ge(most_ready, 1)
            largest = pool.value_load(most[0:1, 0:1], min_val=0, max_val=SEQ)
            with pool.If(largest > P):
                pool.wait_ge(x_tables, 1)
                pool.sem_inc(x_free, 1)
                with pool.Fori(0, NX) as n:
                    need = pool.value_load(over_i[0:1, bass.ds(n, 1)], min_val=0, max_val=1)
                    with pool.If(need > 0):
                        q = pool.value_load(seq_i[0:1, bass.ds(n, 1)], min_val=1, max_val=NX)
                        listed_q = pool.to_reg(q * 3)
                        pool.wait_ge(h1_stored, 16 * NT)
                        pool.wait_ge(x_gidx, listed_q)
                        gather().then_inc(x_rows, 16)
                        pool.wait_ge(acc_stored, 16 * (NT + 1))
                        pool.wait_ge(x_y, q)
                        scatter().then_inc(x_added, 16)
                        pool.wait_ge(x_added, q * 16)
                        pool.sem_inc(x_free, 1)
            pool.sem_inc(x_end, 1)

            for t in range(NT):
                pool.wait_ge(last_gained, t + 1)
                nc.gpsimd.tensor_tensor(h1[:, t, :], h1[:, t, :], wide[:, 2, :], ALU.add).then_inc(last_ready, 1)

        @block.vector
        def _(dve):
            nc.vector.memset(ones16[:], 1.0).then_inc(small_cast, 1)
            nc.vector.memset(place[:], 0.0).then_inc(small_cast, 1)
            nc.vector.memset(value[:], 0.0).then_inc(small_cast, 1)
            dve.wait_ge(consts_landed, 16)
            nc.vector.tensor_copy(tri16[:], cst[:, C_TRI:C_TRI + P]).then_inc(small_cast, 1)
            nc.vector.tensor_copy(three16[:], cst[:, C_ONE3:C_ONE3 + P]).then_inc(small_cast, 1)
            dve.wait_ge(small_cast, 5)
            nc.vector.tensor_copy(value[:, :, 0:E, 0],
                                  cst[:, C_TOK:C_TOK + NT].unsqueeze(2).to_broadcast([P, NT, E])).then_inc(small_cast, 1)

            dve.wait_ge(biases_landed, 32)
            nc.vector.tensor_copy(bpart[:, 0, :], brow).then_inc(bias_step, 1)
            dve.wait_ge(bias_step, 1)
            nc.vector.tensor_tensor(bres, brow, bpart[:, 0, :], ALU.subtract).then_inc(bias_step, 1)
            dve.wait_ge(bias_step, 2)
            nc.vector.tensor_copy(bpart[:, 1, :], bres).then_inc(bias_step, 1)
            dve.wait_ge(bias_step, 3)
            nc.vector.tensor_tensor(brow, bres, bpart[:, 1, :], ALU.subtract).then_inc(bias_step, 1)
            dve.wait_ge(bias_step, 4)
            nc.vector.tensor_copy(bpart[:, 2, :], brow).then_inc(bias_step, 1)

            def residual(t):
                dve.wait_ge(mixed, t + 1)
                dve.wait_ge(wide_landed, 48)
                src = (ps_y if t % 2 == 0 else ps_t)[:].rearrange("p b n -> p (b n)")
                nc.vector.tensor_tensor(z[:, t, :], src, wide[:, 0, :], ALU.mult).then_inc(mix_evacuated, 1)
                dve.wait_ge(mix_evacuated, t + 1)
                nc.vector.scalar_tensor_tensor(out=z[:, t, :], in0=xin[:, t, :], scalar=ALPHA, in1=z[:, t, :],
                                               op0=ALU.mult, op1=ALU.add).then_inc(ln_step, 1)
                dve.wait_ge(ln_step, 3 * t + 1)
                for b in range(2):
                    nc.vector.bn_stats(stats[:, t, b, :], z[:, t, b * BANK:(b + 1) * BANK]).then_inc(ln_step, 1)
                dve.wait_ge(ln_step, 3 * t + 3)
                nc.vector.bn_aggr(mv[:, t, :], stats[:, t, :, :].rearrange("p b n -> p (b n)")).then_inc(stats_ready, 1)
                dve.wait_ge(stats_ready, t + 1)
                nc.vector.tensor_scalar(var[:, t:t + 1], mv[:, t, 1:2], LN_EPS, None, ALU.add).then_inc(var_ready, 1)

            def inverse_root(t, step):
                r, f = rstd[:, t:t + 1], fix[:, t:t + 1]
                nc.vector.reciprocal(r, std[:, t:t + 1]).then_inc(step, 1)
                dve.wait_ge(step, 4 * t + 1)
                nc.vector.scalar_tensor_tensor(out=f, in0=r, scalar=var[:, t:t + 1], in1=r, op0=ALU.mult,
                                               op1=ALU.mult).then_inc(step, 1)
                dve.wait_ge(step, 4 * t + 2)
                nc.vector.tensor_scalar(f, f, -0.5, 1.5, ALU.mult, ALU.add).then_inc(step, 1)
                dve.wait_ge(step, 4 * t + 3)
                nc.vector.tensor_tensor(r, r, f, ALU.mult).then_inc(step, 1)
                dve.wait_ge(step, 4 * t + 4)

            def normalize(t):
                dve.wait_ge(std_ready, t + 1)
                inverse_root(t, rstd_step)
                nc.vector.tensor_scalar(h1[:, t, :], z[:, t, :], mv[:, t, 0:1], rstd[:, t:t + 1],
                                        ALU.subtract, ALU.mult).then_inc(normed, 1)
                dve.wait_ge(normed, t + 1)
                nc.vector.tensor_tensor(h1[:, t, :], h1[:, t, :], wide[:, 1, :], ALU.mult).then_inc(gained, 1)

            for t in range(NT + 1):
                if t < NT:
                    residual(t)
                if t >= 1:
                    normalize(t - 1)

            dve.wait_ge(router_landed, 32)
            for t in range(NT):
                dve.wait_ge(logits_done, t + 1)
                src = (ps_y if t % 2 == 0 else ps_t)[:, 0, 0:E]
                nc.vector.tensor_tensor(logit[:, t, :], src, rb[:], ALU.add).then_inc(logits_read, 1)
                dve.wait_ge(logits_read, t + 1)
                nc.vector.max(top[:, t, :], logit[:, t, :]).then_inc(route_step, 1)
                dve.wait_ge(route_step, 2 * t + 1)
                nc.vector.max_index(topi[:, t, :], top[:, t, :], logit[:, t, :]).then_inc(route_step, 1)
            rs = 2 * NT

            dve.wait_ge(route_step, rs)
            nc.vector.tensor_tensor(gexp[:], top[:, :, 0:TOPK], top[:, :, 0:1].to_broadcast([P, NT, TOPK]),
                                    ALU.subtract).then_inc(exp_in, 1)
            nc.vector.tensor_copy(topf[:], topi[:]).then_inc(route_step, 1)
            dve.wait_ge(route_step, rs + 1)
            experts = cst[:, C_EXP:C_EXP + E].unsqueeze(1).to_broadcast([P, TOPK, E])
            for t in range(NT):
                nc.vector.tensor_tensor(pick[:, t], topf[:, t, 0:TOPK].unsqueeze(2).to_broadcast([P, TOPK, E]),
                                        experts, ALU.is_equal).then_inc(route_step, 1)
            dve.wait_ge(route_step, rs + 1 + NT)
            nc.vector.tensor_reduce(chosen[:], pick.rearrange("p t k e -> p t e k"), AX.X, ALU.add)\
                .then_inc(route_step, 1)
            dve.wait_ge(route_step, rs + 2 + NT)
            nc.vector.tensor_copy(chosen16[:], chosen[:]).then_inc(chosen_ready, 1)
            dve.wait_ge(exp_done, 1)
            nc.vector.tensor_reduce(gsum[:], gexp[:], AX.X, ALU.add).then_inc(route_step, 1)
            dve.wait_ge(route_step, rs + 3 + NT)
            nc.vector.reciprocal(gsum[:], gsum[:]).then_inc(route_step, 1)
            dve.wait_ge(route_step, rs + 4 + NT)
            nc.vector.tensor_tensor(gates[:], gexp[:], gsum[:].unsqueeze(2).to_broadcast([P, NT, TOPK]), ALU.mult)\
                .then_inc(route_step, 1)
            dve.wait_ge(route_step, rs + 5 + NT)
            for t in range(NT):
                nc.vector.tensor_tensor(pickg[:, t], pick[:, t], gates[:, t].unsqueeze(2).to_broadcast([P, TOPK, E]),
                                        ALU.mult).then_inc(route_step, 1)
            dve.wait_ge(route_step, rs + 5 + 2 * NT)
            dve.wait_ge(small_cast, 6)
            nc.vector.tensor_reduce(value[:, :, 0:E, 1], pickg.rearrange("p t k e -> p t e k"), AX.X, ALU.add)\
                .then_inc(place_ready, 1)
            dve.wait_ge(ranked, 1)
            nc.vector.scalar_tensor_tensor(out=place[:, :, 0:E],
                                           in0=ps_y[:, 1, 0:NT * E].rearrange("p (t e) -> p t e", t=NT), scalar=1.0,
                                           in1=chosen[:], op0=ALU.add, op1=ALU.mult).then_inc(place_ready, 1)
            dve.wait_ge(place_ready, 2)

            def one_hot(at):
                return nc.vector.tensor_tensor(
                    hot, at.to_broadcast([P, NT, P]),
                    cst[:, C_SLOT:C_SLOT + P].unsqueeze(1).to_broadcast([P, NT, P]), ALU.is_equal)

            listed = ps_t[:, 0, 0:2]

            one_hot(place[:, :, 0:1]).then_inc(hot_step, 1)
            nc.vector.tensor_copy(val[:], value[:, :, 0, :]).then_inc(hot_step, 1)
            dve.wait_ge(hot_used, 1)
            nc.vector.tensor_copy(slot[:, 0, :], listed).then_inc(gidx_ready, 1)
            nc.vector.tensor_scalar(sidx_all[:, 0:1], listed[:, 0:1], float(ABSENT), cst[:, C_SPARE:C_SPARE + 1],
                                    ALU.add, ALU.min).then_inc(gidx_ready, 1)
            nc.vector.tensor_scalar(gidx[:], listed[:, 0:1], float(ABSENT), None, ALU.add).then_inc(gidx_ready, 1)

            nc.vector.tensor_copy(count[:], ps_t[0:1, 1, 0:E]).then_inc(route_step, 1)
            dve.wait_ge(route_step, rs + 6 + 2 * NT)
            nc.vector.tensor_reduce(most[:], count[:], AX.X, ALU.max).then_inc(most_ready, 1)

            def clamp_gate():
                return nc.vector.tensor_scalar(gate, ps_gu[:, 0:2, :].rearrange("p b n -> p (b n)"), LIMIT, None,
                                               ALU.min)

            def clamp_up():
                return nc.vector.tensor_scalar(up, ps_gu[:, 2:4, :].rearrange("p b n -> p (b n)"), LIMIT, -LIMIT,
                                               ALU.min, ALU.max)

            def up_gate():
                return nc.vector.scalar_tensor_tensor(out=up, in0=up, scalar=1.0, in1=gate,
                                                      op0=ALU.add, op1=ALU.mult)

            def hidden():
                return nc.vector.tensor_tensor(hid, up, sig, ALU.mult)

            one_hot(place[:, :, 1:2]).then_inc(hot_step, 1)
            nc.vector.tensor_copy(val[:], value[:, :, 1, :]).then_inc(hot_step, 1)
            dve.wait_ge(hot_used, 2)
            dve.wait_ge(xg_landed, 16)
            nc.vector.tensor_copy(slot[:, 1, :], listed).then_inc(gidx_ready, 1)
            nc.vector.tensor_scalar(sidx_all[:, 1:2], listed[:, 0:1], float(ABSENT), cst[:, C_SPARE:C_SPARE + 1],
                                    ALU.add, ALU.min).then_inc(gidx_ready, 1)
            nc.vector.tensor_scalar(gidx[:], listed[:, 0:1], float(ABSENT), None, ALU.add).then_inc(gidx_ready, 1)
            dve.wait_ge(acc_stored, 16 * (NT + 1))
            dve.wait_ge(gu_used, KD)
            clamp_gate().then_inc(gate_ready, 1)
            clamp_up().then_inc(up_ready, 1)
            dve.wait_ge(gate_ready, 1)
            dve.wait_ge(up_ready, 1)
            up_gate().then_inc(act_step, 1)
            dve.wait_ge(act_step, 1)
            dve.wait_ge(sig_ready, 1)
            hidden().then_inc(hid_ready, 1)
            with dve.Fori(1, E) as e:
                one_hot(place[:, :, bass.ds(e + 1, 1)]).then_inc(hot_step, 1)
                nc.vector.tensor_copy(val[:], value[:, :, bass.ds(e + 1, 1), :].rearrange("p t o c -> p t (o c)"))\
                    .then_inc(hot_step, 1)
                dve.wait_ge(hot_used, e + 2)
                dve.wait_ge(xg_landed, e * 16 + 16)
                nc.vector.tensor_copy(slot[:, bass.ds(e + 1, 1), :].rearrange("p o c -> p (o c)"), listed)\
                    .then_inc(gidx_ready, 1)
                nc.vector.tensor_scalar(sidx_all[:, bass.ds(e + 1, 1)], listed[:, 0:1], float(ABSENT),
                                        cst[:, C_SPARE:C_SPARE + 1], ALU.add, ALU.min).then_inc(gidx_ready, 1)
                nc.vector.tensor_scalar(gidx[:], listed[:, 0:1], float(ABSENT), None, ALU.add).then_inc(gidx_ready, 1)
                dve.wait_ge(gu_used, e * KD + KD)
                clamp_gate().then_inc(gate_ready, 1)
                clamp_up().then_inc(up_ready, 1)
                dve.wait_ge(gate_ready, e + 1)
                dve.wait_ge(up_ready, e + 1)
                up_gate().then_inc(act_step, 1)
                dve.wait_ge(act_step, e + 1)
                dve.wait_ge(sig_ready, e + 1)
                hidden().then_inc(hid_ready, 1)

            dve.wait_ge(most_ready, 1)
            largest = dve.value_load(most[0:1, 0:1], min_val=0, max_val=SEQ)
            with dve.If(largest > P):
                for j in range(MORE):
                    nc.vector.tensor_scalar(over[:, j * E:(j + 1) * E], count[:], float(P * (j + 1)), None, ALU.is_gt)\
                        .then_inc(x_step, 1)
                    nc.vector.tensor_scalar(place_x[:, :, j * E:(j + 1) * E], place[:, :, 0:E], float(-P * (j + 1)),
                                            None, ALU.add).then_inc(x_step, 1)
                dve.wait_ge(x_step, 2 * MORE)
                nc.vector.tensor_tensor_scan(seq_f[:], over[:], over[:], 0.0, ALU.add, ALU.max).then_inc(x_step, 1)
                nc.vector.tensor_copy(over_i[:], over[:]).then_inc(x_step, 1)
                dve.wait_ge(x_step, 2 * MORE + 2)
                nc.vector.tensor_copy(seq_i[:], seq_f[:]).then_inc(x_tables, 1)
                dve.wait_ge(x_tables, 1)
                for j in range(MORE):
                    with dve.Fori(0, E) as e:
                        need = dve.value_load(over_i[0:1, bass.ds(e + j * E, 1)], min_val=0, max_val=1)
                        with dve.If(need > 0):
                            q = dve.value_load(seq_i[0:1, bass.ds(e + j * E, 1)], min_val=1, max_val=NX)
                            dve.wait_ge(x_free, q)
                            one_hot(place_x[:, :, bass.ds(e + j * E, 1)]).then_inc(x_hot, 1)
                            nc.vector.tensor_copy(
                                val[:], value[:, :, bass.ds(e, 1), :].rearrange("p t o c -> p t (o c)"))\
                                .then_inc(x_hot, 1)
                            dve.wait_ge(x_listed, q)
                            nc.vector.tensor_copy(slot_x[:], listed).then_inc(x_gidx, 1)
                            nc.vector.tensor_scalar(sidx[:], listed[:, 0:1], float(ABSENT),
                                                    cst[:, C_SPARE:C_SPARE + 1], ALU.add, ALU.min).then_inc(x_gidx, 1)
                            nc.vector.tensor_scalar(gidx[:], listed[:, 0:1], float(ABSENT), None, ALU.add)\
                                .then_inc(x_gidx, 1)
                            dve.wait_ge(x_gu, q)
                            clamp_gate().then_inc(x_gate, 1)
                            clamp_up().then_inc(x_up, 1)
                            dve.wait_ge(x_gate, q)
                            dve.wait_ge(x_up, q)
                            up_gate().then_inc(x_upgate, 1)
                            dve.wait_ge(x_upgate, q)
                            dve.wait_ge(x_sig, q)
                            hidden().then_inc(x_hid, 1)

            dve.wait_ge(wide2_landed, 32)
            for t in range(NT + 1):
                if t < NT:
                    dve.wait_ge(sums_landed[t], 16)
                    for b in range(2):
                        nc.vector.bn_stats(stats[:, t, b, :], xin[:, t, b * BANK:(b + 1) * BANK]).then_inc(last_step, 1)
                    dve.wait_ge(last_step, 2 * t + 2)
                    nc.vector.bn_aggr(mv[:, t, :], stats[:, t, :, :].rearrange("p b n -> p (b n)"))\
                        .then_inc(last_stats, 1)
                    dve.wait_ge(last_stats, t + 1)
                    nc.vector.tensor_scalar(var[:, t:t + 1], mv[:, t, 1:2], LN_EPS, None, ALU.add)\
                        .then_inc(last_var, 1)
                if t >= 1:
                    dve.wait_ge(last_std, t)
                    inverse_root(t - 1, last_rstd)
                    nc.vector.tensor_scalar(h1[:, t - 1, :], xin[:, t - 1, :], mv[:, t - 1, 0:1], rstd[:, t - 1:t],
                                            ALU.subtract, ALU.mult).then_inc(last_normed, 1)
                    dve.wait_ge(last_normed, t)
                    nc.vector.tensor_tensor(h1[:, t - 1, :], h1[:, t - 1, :], wide[:, 1, :], ALU.mult)\
                        .then_inc(last_gained, 1)

        @block.tensor
        def _(pe):
            pe.wait_ge(consts_landed, 16)

            def pool_rows(t):
                pe.wait_ge(x_landed[t], 16)
                if t == 0:
                    pe.wait_ge(meta_landed, 16)
                if t >= 2:
                    pe.wait_ge(pooled_copied, t - 1)
                before = prev[:, :] if t == 0 else xin[:, t - 1, :]
                for c in range(KD):
                    dst = ps_gu[:, 2 * (t % 2) + c // 4, (c % 4) * P:(c % 4 + 1) * P]
                    band = cst[:, C_BAND + (c // 2) * 2 * P:C_BAND + (c // 2 + 1) * 2 * P]
                    cols = slice(c * P, (c + 1) * P)
                    nc.tensor.matmul(dst, xin[:, t, cols], band[:, 0:P], start=True, stop=False)
                    last = nc.tensor.matmul(dst, before[:, cols], band[:, P:2 * P], start=False, stop=True)
                last.then_inc(pooled, 1)

            def mix_rows(t):
                pe.wait_ge(pooled_copied, t + 1)
                pe.wait_ge(pw_landed, 16)
                if t >= 2:
                    pe.wait_ge(mix_evacuated, t - 1)
                dst = (ps_y if t % 2 == 0 else ps_t)[:].rearrange("p b n -> p (b n)")
                for g in range(NG):
                    for k in range(2):
                        last = nc.tensor.matmul(dst[:, g * GW:(g + 1) * GW], turned[:, t % 2, 2 * g + k, :],
                                                pw[:, 2 * g + k, :], start=(k == 0), stop=(k == 1))
                last.then_inc(mixed, 1)

            for t in range(NT + 1):
                if t < NT:
                    pool_rows(t)
                if t >= 1:
                    mix_rows(t - 1)

            pe.wait_ge(router_landed, 32)
            for t in range(NT):
                pe.wait_ge(h1_ready, t + 1)
                pe.wait_ge(pooled_copied, NT)
                if t >= 2:
                    pe.wait_ge(h1_copied, t - 1)
                turn(ps_gu[:, 2 * (t % 2):2 * (t % 2) + 2, :], h1[:, t, :]).then_inc(h1_turned, 1)
                pe.wait_ge(h1_copied, t + 1)
                pe.wait_ge(mix_evacuated, NT)
                if t >= 2:
                    pe.wait_ge(logits_read, t - 1)
                dst = (ps_y if t % 2 == 0 else ps_t)[:, 0, 0:E]
                for k in range(KD):
                    last = nc.tensor.matmul(dst, turned[:, t % 2, k, :], rwt[:, k, :], start=(k == 0),
                                            stop=(k == KD - 1))
                last.then_inc(logits_done, 1)

            pe.wait_ge(chosen_ready, 1)
            pe.wait_ge(small_cast, 6)
            rank = ps_y[:, 1, 0:NT * E]
            for t in range(NT):
                dst = rank[:, t * E:(t + 1) * E]
                for s in range(t):
                    nc.tensor.matmul(dst, ones16[:], chosen16[:, s, :], start=(s == 0), stop=False)
                nc.tensor.matmul(dst, tri16[:], chosen16[:, t, :], start=(t == 0), stop=True)
            for t in range(NT):
                last = nc.tensor.matmul(ps_t[:, 1, 0:E], ones16[:], chosen16[:, t, :], start=(t == 0),
                                        stop=(t == NT - 1))
            last.then_inc(ranked, 1)

            listed = ps_t[:, 0, 0:2]
            pe.wait_ge(hot_step, 2)
            pe.wait_ge(logits_read, NT)
            list_slots(listed).then_inc(hot_used, 1)
            pe.wait_ge(xg_landed, 16)
            pe.wait_ge(most_ready, 1)
            turn(ps_t, xg).then_inc(xg_turned, 1)

            pe.wait_ge(gub_landed, 16)
            gate_up_bias().then_inc(gub_used, 1)
            pe.wait_ge(xt_ready, 1)
            for k in range(KD):
                pe.wait_ge(gu_landed[k], 16)
                last = gate_up(k)
                last.then_inc(gu_used, 1)
                if k == 1:
                    pe.wait_ge(hot_step, 4)
                    list_slots(listed).then_inc(hot_used, 1)
            pe.wait_ge(xg_landed, 32)
            turn(ps_t, xg).then_inc(xg_turned, 1)
            pe.wait_ge(hid_ready, 1)
            pe.wait_ge(xt_ready, 2)
            turn(ps_t, hid).then_inc(hid_turned, 1)
            with pe.Fori(1, E) as e:
                pe.wait_ge(gub_landed, e * 16 + 16)
                pe.wait_ge(up_ready, e)
                pe.wait_ge(gate_ready, e)
                gate_up_bias().then_inc(gub_used, 1)
                pe.wait_ge(xt_ready, e + 1)
                for k in range(KD):
                    pe.wait_ge(gu_landed[k], e * 16 + 16)
                    gate_up(k).then_inc(gu_used, 1)
                    if k == 1:
                        pe.wait_ge(hot_step, e * 2 + 4)
                        pe.wait_ge(ht_ready, e)
                        list_slots(listed).then_inc(hot_used, 1)
                pe.wait_ge(xg_landed, e * 16 + 32)
                turn(ps_t, xg).then_inc(xg_turned, 1)
                pe.wait_ge(db_landed, e * 16)
                pe.wait_ge(ht_ready, e)
                down_bias().then_inc(db_used, 1)
                for k in range(KD):
                    if k % 2 == 0:
                        pe.wait_ge(wd_landed[k // 2], e * 16)
                    last = down(k)
                    if k % 2 == 1:
                        last.then_inc(wd_used, 1)
                pe.wait_ge(hid_ready, e + 1)
                pe.wait_ge(xt_ready, e + 2)
                turn(ps_t, hid).then_inc(hid_turned, 1)
            pe.wait_ge(db_landed, E * 16)
            pe.wait_ge(y_ready, E - 1)
            pe.wait_ge(ht_ready, E)
            down_bias()
            for k in range(KD):
                if k % 2 == 0:
                    pe.wait_ge(wd_landed[k // 2], E * 16)
                last = down(k)
                if k % 2 == 1:
                    last.then_inc(wd_used, 1)

            largest = pe.value_load(most[0:1, 0:1], min_val=0, max_val=SEQ)
            with pe.If(largest > P):
                pe.wait_ge(x_tables, 1)
                with pe.Fori(0, NX) as n:
                    need = pe.value_load(over_i[0:1, bass.ds(n, 1)], min_val=0, max_val=1)
                    with pe.If(need > 0):
                        q = pe.value_load(seq_i[0:1, bass.ds(n, 1)], min_val=1, max_val=NX)
                        pe.wait_ge(x_hot, q * 2)
                        list_slots(listed).then_inc(x_listed, 1)
                        pe.wait_ge(x_rows, q * 16)
                        turn(ps_t, xg).then_inc(x_turned, 1)
                        pe.wait_ge(x_weights, q * (16 * (KD + 3)))
                        pe.wait_ge(x_xt, q)
                        gate_up_bias()
                        for k in range(KD):
                            last = gate_up(k)
                        last.then_inc(x_gu, 1)
                        pe.wait_ge(x_hid, q)
                        turn(ps_t, hid).then_inc(x_hturned, 1)
                        pe.wait_ge(x_ht, q)
                        down_bias()
                        for k in range(KD):
                            last = down(k)
                        last.then_inc(x_d, 1)


_INS = ["x", "meta_tokens", "consts", "pool_w", "pool_scale", "router_wt", "router_b", "moe_wgu", "moe_bgu",
        "moe_wd", "moe_bd", "ln_g", "ln_b"]


def kernel(**inputs):
    import concourse.bacc as bacc
    from concourse.bass_utils import run_bass_kernel_spmd

    given = {n: np.ascontiguousarray(a) for n, a in inputs.items()}
    given["consts"] = shape_constants()
    given["router_wt"] = np.ascontiguousarray(given["router_w"][0].T)
    given["moe_wgu"] = given["moe_wgu"][0]
    given["moe_wd"] = given["moe_wd"][0]
    nc = bacc.Bacc("TRN2", target_bir_lowering=False, num_devices=1)
    arrays, args = {}, []
    for name in _INS:
        a = given[name]
        arrays[f"in_{name}"] = a
        args.append(nc.dram_tensor(f"in_{name}", a.shape, mybir.dt.from_np(a.dtype), kind="ExternalInput").ap())
    out = nc.dram_tensor("out_rows", (1, SEQ, D), F32, kind="ExternalOutput").ap()
    trunk(nc, *args, out)
    return run_bass_kernel_spmd(nc, [arrays], core_ids=[0]).results[0]["out_rows"]
```

```python
from contextlib import ExitStack

import numpy as np

import concourse.bass as bass
from concourse import mybir

P = 128
SEQ, D, META = 512, 1024, 16
NT = SEQ // P
KD = D // P
WINDOWS = (2, 4, 8, 16)
NG = len(WINDOWS)
GW = D // NG
E, TOPK, F = 32, 4, 1024
BANK = 512
NB = 3
ALPHA = 2.0 ** 0.25
LN_EPS = 1e-5
LIMIT, SWISH = 7.0, 1.702
EP = E + 1
BQ = 2 * F // 4
ABSENT = 4096
MORE = SEQ // P - 1
NX = MORE * E

F32, F32R, BF16 = mybir.dt.float32, mybir.dt.float32r, mybir.dt.bfloat16
I32, U32 = mybir.dt.int32, mybir.dt.uint32
ALU, ACT, AX = mybir.AluOpType, mybir.ActivationFunctionType, mybir.AxisListType

GU, DN = 0, 1
UNITS = [(GU, k) for k in range(KD)] + [(DN, j) for j in range(KD // 2)]
WHOLE = [(GU, 2), (GU, 5), (DN, 1)]
SPLIT = [u for u in UNITS if u not in WHOLE]
RING = 3
SG, SA = sum(u[0] == GU for u in SPLIT), len(SPLIT)
WG, WA = len(UNITS[:KD]) - SG, len(WHOLE)
UW = 2 * F
assert SA % RING == 0 and (GU, KD - 1) in SPLIT and (DN, KD // 2 - 1) in SPLIT


def nth(e, unit):
    like, gates_up, both = (SPLIT, SG, SA) if unit in SPLIT else (WHOLE, WG, WA)
    i = like.index(unit)
    if isinstance(e, int) and e == 0:
        return i
    if isinstance(e, int) and e == E:
        return gates_up + both * (E - 1) + i - gates_up
    return e * both + (gates_up - both + i)


def ring_slot(e, unit):
    i = SPLIT.index(unit)
    if isinstance(e, int) and e in (0, E):
        return (nth(e, unit)) % RING
    return (SG + i) % RING


C_ID = 0
C_SLOT = C_ID + P
C_EXP = C_SLOT + P
C_TOK = C_EXP + E
C_SPARE = C_TOK + NT
C_ALL = C_SPARE + 1
M_BAND = 0
M_TRI = M_BAND + NG * 2 * P
M_ONE3 = M_TRI + P
M_ALL = M_ONE3 + P


def shape_constants():
    c, m = np.zeros((P, C_ALL), np.float32), np.zeros((P, M_ALL), np.float32)
    i = np.arange(P)
    s, t = i[:, None], i[None, :]
    c[:, C_ID:C_ID + P] = np.eye(P)
    c[:, C_SLOT:C_SLOT + P] = i + 1
    c[:, C_EXP:C_EXP + E] = np.arange(E)
    c[:, C_TOK:C_TOK + NT] = i[:, None] + P * np.arange(NT) - ABSENT
    c[:, C_SPARE] = SEQ + i
    for g, win in enumerate(WINDOWS):
        own = ((s <= t) & (s > t - win)) / win - (s == t)
        before = (s - P > t - win) / win
        at = M_BAND + g * 2 * P
        m[:, at:at + P], m[:, at + P:at + 2 * P] = own, before
    m[:, M_TRI:M_TRI + P] = s < t
    m[:NB, M_ONE3:M_ONE3 + P] = 1
    return c, m


def trunk(nc, x, meta, consts, masks, pool_w, pool_scale, router_wt, router_b, wgu, bgu, wd, bd, ln_g, ln_b, out):
    ctx = ExitStack()
    with ctx:
        def sb(name, shape, dt=F32):
            return ctx.enter_context(nc.sbuf_tensor(name, shape, dt))

        def sem(name):
            return ctx.enter_context(nc.semaphore(name))

        h1_dram = nc.dram_tensor("h1_rows", [SEQ, D], F32, kind="Internal").ap()
        acc_dram = nc.dram_tensor("acc_rows", [SEQ + P, D], F32, kind="Internal").ap()
        gub_dram = nc.dram_tensor("gu_bias_parts", [NB, E, 2 * F], BF16, kind="Internal").ap()
        db_dram = nc.dram_tensor("d_bias_parts", [NB, E, D], BF16, kind="Internal").ap()

        cst = sb("cst", [P, C_ALL])
        gu_ring = sb("gu_ring", [P, KD, 2 * F])
        wd_ring = sb("wd_ring", [P, KD, D])
        rb = sb("rb", [P, E])
        stats = sb("stats", [P, NT, 2, 6])
        mv = sb("mv", [P, NT, 2])
        var = sb("var", [P, NT])
        std = sb("std", [P, NT])
        rstd = sb("rstd", [P, NT])
        fix = sb("fix", [P, NT])
        logit = sb("logit", [P, NT, E])
        top = sb("top", [P, NT, 8])
        topi = sb("topi", [P, NT, 8], U32)
        topf = sb("topf", [P, NT, 8])
        gexp = sb("gexp", [P, NT, TOPK])
        gsum = sb("gsum", [P, NT])
        gates = sb("gates", [P, NT, TOPK])
        chosen = sb("chosen", [P, NT, E])
        chosen16 = sb("chosen16", [P, NT, E], BF16)
        place = sb("place", [P, NT, EP])
        value = sb("value", [P, NT, EP, 2])
        tri16 = sb("tri16", [P, P], BF16)
        ones16 = sb("ones16", [P, P], BF16)
        three16 = sb("three16", [P, P], BF16)
        count = sb("count", [1, E])
        most = sb("most", [1, 1], I32)
        hot = sb("hot", [P, NT, P])
        val = sb("val", [P, NT, 2])
        slot = sb("slot", [P, EP, 2])
        gidx = sb("gidx", [P, 1], I32)
        sidx_all = sb("sidx_all", [P, EP], I32)
        sidx = sb("sidx", [P, 1], I32)
        gu_bias = sb("gu_bias", [P, 2 * F], BF16)
        d_bias = sb("d_bias", [P, D], BF16)
        place_x = sb("place_x", [P, NT, NX])
        over = sb("over", [1, NX])
        seq_f = sb("seq_f", [1, NX])
        over_i = sb("over_i", [1, NX], I32)
        seq_i = sb("seq_i", [1, NX], I32)
        slot_x = sb("slot_x", [P, 2])

        with ExitStack() as early:
            def sb_early(name, shape, dt=F32):
                return early.enter_context(nc.sbuf_tensor(name, shape, dt))

            xin = sb_early("xin", [P, NT, D])
            wide = sb_early("wide", [P, 3, D])
            prev = sb_early("prev", [P, D])
            pw = sb_early("pw", [P, NG * 2, GW])
            msk = sb_early("msk", [P, M_ALL])
            turned = sb_early("turned", [P, 2, KD, P])
            bpart = sb_early("bpart", [P, NB, BQ + D // 4], BF16)
            rwt = sb_early("rwt", [P, KD, E])
            z = sb_early("z", [P, NT, D])
            h1 = sb_early("h1", [P, NT, D])
        brow, bres = z[:, 2, 0:BQ + D // 4], z[:, 3, 0:BQ + D // 4]
        pick = turned[:, 0].rearrange("p k n -> p (k n)")[:, 0:NT * TOPK * E]\
            .rearrange("p (t k e) -> p t k e", t=NT, k=TOPK)
        pickg = turned[:, 0].rearrange("p k n -> p (k n)")[:, NT * TOPK * E:]\
            .rearrange("p (t k e) -> p t k e", t=NT, k=TOPK)

        high = sb("high", [P, RING, UW], F32R)
        low = sb("low", [P, RING, UW], F32R)
        xt_high = sb("xt_high", [P, KD, P], F32R)
        xt_low = sb("xt_low", [P, KD, P], F32R)
        ht_high = sb("ht_high", [P, KD, P], F32R)
        ht_low = sb("ht_low", [P, KD, P], F32R)
        xt = sb("xt", [P, KD, P])
        ht = sb("ht", [P, KD, P])
        gate = sb("gate", [P, F])
        sig = sb("sig", [P, F])
        up = sb("up", [P, F])
        xg = sb("xg", [P, D])
        y = sb("y", [P, D])

        ident = cst[:, C_ID:C_ID + P]

        ps_gu = ctx.enter_context(nc.psum_tensor("ps_gu", [P, 4, BANK], F32))
        ps_y = ctx.enter_context(nc.psum_tensor("ps_y", [P, 2, BANK], F32))
        ps_t = ctx.enter_context(nc.psum_tensor("ps_t", [P, 2, BANK], F32))

        x_landed = [sem(f"x_landed{t}") for t in range(NT)]
        consts_landed = sem("consts_landed")
        meta_cleared = sem("meta_cleared")
        meta_landed = sem("meta_landed")
        pw_landed = sem("pw_landed")
        wide_landed = sem("wide_landed")
        router_landed = sem("router_landed")
        biases_landed = sem("biases_landed")
        pooled = sem("pooled")
        pooled_copied = sem("pooled_copied")
        mixed = sem("mixed")
        mix_evacuated = sem("mix_evacuated")
        ln_step = sem("ln_step")
        stats_ready = sem("stats_ready")
        var_ready = sem("var_ready")
        std_ready = sem("std_ready")
        rstd_step = sem("rstd_step")
        normed = sem("normed")
        gained = sem("gained")
        h1_ready = sem("h1_ready")
        h1_scaled = sem("h1_scaled")
        h1_stored = sem("h1_stored")
        acc_stored = sem("acc_stored")
        h1_turned = sem("h1_turned")
        h1_copied = sem("h1_copied")
        logits_done = sem("logits_done")
        logits_read = sem("logits_read")
        bias_step = sem("bias_step")
        bias_stored = sem("bias_stored")
        zeros_set = sem("zeros_set")
        small_cast = sem("small_cast")
        route_step = sem("route_step")
        exp_in = sem("exp_in")
        exp_done = sem("exp_done")
        chosen_ready = sem("chosen_ready")
        ranked = sem("ranked")
        place_ready = sem("place_ready")
        most_ready = sem("most_ready")
        gu_landed = [sem(f"gu_landed{k}") for k in range(KD)]
        wd_landed = [sem(f"wd_landed{k}") for k in range(KD // 2)]
        high_ready = sem("high_ready")
        low_ready = sem("low_ready")
        split_used = sem("split_used")
        whole_used = sem("whole_used")
        gub_landed = sem("gub_landed")
        gub_used = sem("gub_used")
        db_landed = sem("db_landed")
        db_used = sem("db_used")
        hot_step = sem("hot_step")
        hot_used = sem("hot_used")
        gidx_ready = sem("gidx_ready")
        xg_landed = sem("xg_landed")
        xg_turned = sem("xg_turned")
        xt_high_ready = sem("xt_high_ready")
        xt_low_ready = sem("xt_low_ready")
        xt_whole_ready = sem("xt_whole_ready")
        act_step = sem("act_step")
        gate_ready = sem("gate_ready")
        up_ready = sem("up_ready")
        y_free = sem("y_free")
        sig_ready = sem("sig_ready")
        hid_ready = sem("hid_ready")
        hid_turned = sem("hid_turned")
        ht_high_ready = sem("ht_high_ready")
        ht_low_ready = sem("ht_low_ready")
        ht_whole_ready = sem("ht_whole_ready")
        y_ready = sem("y_ready")
        sidx_ready = sem("sidx_ready")
        rows_added = sem("rows_added")
        x_tables = sem("x_tables")
        x_step = sem("x_step")
        x_free = sem("x_free")
        x_weights = sem("x_weights")
        x_hot = sem("x_hot")
        x_listed = sem("x_listed")
        x_gidx = sem("x_gidx")
        x_rows = sem("x_rows")
        x_turned = sem("x_turned")
        x_xt = sem("x_xt")
        x_gu = sem("x_gu")
        x_gate = sem("x_gate")
        x_up = sem("x_up")
        x_upgate = sem("x_upgate")
        x_sig = sem("x_sig")
        x_hid = sem("x_hid")
        x_hturned = sem("x_hturned")
        x_ht = sem("x_ht")
        x_d = sem("x_d")
        x_y = sem("x_y")
        x_added = sem("x_added")
        x_end = sem("x_end")
        wide2_landed = sem("wide2_landed")
        sums_landed = [sem(f"sums_landed{t}") for t in range(NT)]
        last_step = sem("last_step")
        last_stats = sem("last_stats")
        last_var = sem("last_var")
        last_std = sem("last_std")
        last_rstd = sem("last_rstd")
        last_normed = sem("last_normed")
        last_gained = sem("last_gained")
        last_ready = sem("last_ready")
        out_stored = sem("out_stored")

        wgu_v = wgu.rearrange("e (k p) n -> e p k n", p=P)
        wd_v = wd.rearrange("e (k p) n -> e p k n", p=P)

        def turn(dst, src):
            for k in range(KD):
                last = nc.tensor.transpose(dst[:, k // 4, (k % 4) * P:(k % 4 + 1) * P],
                                           src[:, k * P:(k + 1) * P], ident)
            return last

        def gate_up_bias():
            for n in range(4):
                last = nc.tensor.matmul(ps_gu[:, n, :], three16[:], gu_bias[:, n * BANK:(n + 1) * BANK],
                                        start=True, stop=False)
            return last

        def gate_up(k):
            for n in range(4):
                last = nc.tensor.matmul(ps_gu[:, n, :], xt[:, k, :], gu_ring[:, k, n * BANK:(n + 1) * BANK],
                                        start=False, stop=(k == KD - 1))
            return last

        def gate_up_parts(k, s):
            for n in range(4):
                cols = slice(n * BANK, (n + 1) * BANK)
                nc.tensor.matmul(ps_gu[:, n, :], xt_high[:, k, :], high[:, s, cols], start=False, stop=False)
                nc.tensor.matmul(ps_gu[:, n, :], xt_high[:, k, :], low[:, s, cols], start=False, stop=False)
            for n in range(4):
                last = nc.tensor.matmul(ps_gu[:, n, :], xt_low[:, k, :], high[:, s, n * BANK:(n + 1) * BANK],
                                        start=False, stop=(k == KD - 1))
            return last

        def down_bias():
            for n in range(2):
                last = nc.tensor.matmul(ps_y[:, n, :], three16[:], d_bias[:, n * BANK:(n + 1) * BANK],
                                        start=True, stop=False)
            return last

        def down(k):
            for n in range(2):
                last = nc.tensor.matmul(ps_y[:, n, :], ht[:, k, :], wd_ring[:, k, n * BANK:(n + 1) * BANK],
                                        start=False, stop=(k == KD - 1))
            return last

        def down_parts(j, s):
            for k in (2 * j, 2 * j + 1):
                for n in range(2):
                    at = (k % 2) * D + n * BANK
                    nc.tensor.matmul(ps_y[:, n, :], ht_high[:, k, :], high[:, s, at:at + BANK],
                                     start=False, stop=False)
                    nc.tensor.matmul(ps_y[:, n, :], ht_high[:, k, :], low[:, s, at:at + BANK],
                                     start=False, stop=False)
                for n in range(2):
                    at = (k % 2) * D + n * BANK
                    last = nc.tensor.matmul(ps_y[:, n, :], ht_low[:, k, :], high[:, s, at:at + BANK],
                                            start=False, stop=(k == KD - 1))
            return last

        def raw(unit):
            kind, i = unit
            return gu_ring[:, i, :] if kind == GU else wd_ring[:, 2 * i:2 * i + 2, :].rearrange("p k n -> p (k n)")

        def list_slots(bank):
            for t in range(NT):
                last = nc.tensor.matmul(bank, hot[:, t, :], val[:, t, :], start=(t == 0), stop=(t == NT - 1))
            return last

        block = ctx.enter_context(nc.Block())

        @block.sync
        def _(sp):
            for t in range(NT):
                sp.dma_start(xin[:, t, :], x[0, t * P:(t + 1) * P, :]).then_inc(x_landed[t], 16)
                if t == 0:
                    sp.dma_start(msk[:], masks).then_inc(consts_landed, 16)
                    sp.dma_start(cst[:], consts).then_inc(consts_landed, 16)
            sp.dma_start(pw[:], pool_w[0].rearrange("g (k p) n -> p (g k) n", p=P)).then_inc(pw_landed, 16)

            def load_gu(e, k):
                sp.dma_start(gu_ring[:, k, :], wgu_v[e, :, k, :]).then_inc(gu_landed[k], 16)

            def load_wd(e, k2):
                sp.dma_start(wd_ring[:, 2 * k2:2 * k2 + 2, :], wd_v[e, :, 2 * k2:2 * k2 + 2, :])\
                    .then_inc(wd_landed[k2], 16)

            def load_gu_bias(e):
                sp.dma_start(gu_bias[0:NB, :], gub_dram[:, e, :]).then_inc(gub_landed, 16)

            def load_d_bias(e):
                sp.dma_start(d_bias[0:NB, :], db_dram[:, e, :]).then_inc(db_landed, 16)

            def reuse(e, unit):
                if unit in SPLIT:
                    sp.wait_ge(low_ready, nth(e, unit) + 1)
                else:
                    sp.wait_ge(whole_used, nth(e, unit) + 1)

            for k in range(KD):
                load_gu(0, k)
            for j in range(KD // 2):
                load_wd(0, j)
            sp.wait_ge(bias_stored, 32 * NB)
            sp.wait_ge(zeros_set, 2)
            load_gu_bias(0)
            load_d_bias(0)
            sp.wait_ge(gub_used, 1)
            load_gu_bias(1)
            for k in range(KD):
                reuse(0, (GU, k))
                load_gu(1, k)

            def ahead(e):
                sp.wait_ge(gub_used, e)
                load_gu_bias(e)
                for k in range(KD):
                    reuse(e - 1, (GU, k))
                    load_gu(e, k)
                sp.wait_ge(db_used, e - 1)
                load_d_bias(e - 1)
                for j in range(KD // 2):
                    reuse(e - 1, (DN, j))
                    load_wd(e - 1, j)

            ahead(2)
            with sp.Fori(3, E) as e:
                ahead(e)
            sp.wait_ge(db_used, E - 1)
            load_d_bias(E - 1)
            for j in range(KD // 2):
                reuse(E - 1, (DN, j))
                load_wd(E - 1, j)

            sp.wait_ge(split_used, nth(E, (DN, KD // 2 - 1)) + 1)
            sp.dma_start(wide[:, 1, :], ln_g[0, 1].partition_broadcast(P)).then_inc(wide2_landed, 16)
            sp.dma_start(wide[:, 2, :], ln_b[0, 1].partition_broadcast(P)).then_inc(wide2_landed, 16)

            sp.wait_ge(most_ready, 1)
            largest = sp.value_load(most[0:1, 0:1], min_val=0, max_val=SEQ)
            with sp.If(largest > P):
                sp.wait_ge(x_tables, 1)
                for j in range(MORE):
                    with sp.Fori(0, E) as e:
                        need = sp.value_load(over_i[0:1, bass.ds(e + j * E, 1)], min_val=0, max_val=1)
                        with sp.If(need > 0):
                            q = sp.value_load(seq_i[0:1, bass.ds(e + j * E, 1)], min_val=1, max_val=NX)
                            sp.wait_ge(x_free, q)
                            sp.dma_start(gu_bias[0:NB, :], gub_dram[:, e, :]).then_inc(x_weights, 16)
                            sp.dma_start(d_bias[0:NB, :], db_dram[:, e, :]).then_inc(x_weights, 16)
                            for k in range(KD):
                                sp.dma_start(gu_ring[:, k, :], wgu_v[e, :, k, :]).then_inc(x_weights, 16)
                            sp.dma_start(wd_ring[:], wd_v[e]).then_inc(x_weights, 16)

            sp.wait_ge(x_end, 1)
            for t in range(NT):
                sp.dma_start(xin[:, t, :], acc_dram[t * P:(t + 1) * P, :]).then_inc(sums_landed[t], 16)
            for t in range(NT):
                sp.wait_ge(last_ready, t + 1)
                sp.dma_start(out[0, t * P:(t + 1) * P, :], h1[:, t, :]).then_inc(out_stored, 16)
            sp.wait_ge(out_stored, 16 * NT)

        @block.scalar
        def _(act):
            act.dma_start(wide[:, 0, :], pool_scale[0].partition_broadcast(P)).then_inc(wide_landed, 16)
            act.wait_ge(meta_cleared, 1)
            act.dma_start(prev[P - META:P, :], meta).then_inc(meta_landed, 16)
            act.dma_start(brow[:, 0:BQ], bgu[0].rearrange("e (q n) -> (e q) n", q=4)).then_inc(biases_landed, 16)
            act.dma_start(brow[:, BQ:], bd[0].rearrange("e (q n) -> (e q) n", q=4)).then_inc(biases_landed, 16)
            act.dma_start(wide[:, 1, :], ln_g[0, 0].partition_broadcast(P)).then_inc(wide_landed, 16)
            act.dma_start(wide[:, 2, :], ln_b[0, 0].partition_broadcast(P)).then_inc(wide_landed, 16)
            act.dma_start(rwt[:], router_wt.rearrange("(k p) e -> p k e", p=P)).then_inc(router_landed, 16)
            act.dma_start(rb[:], router_b[0].partition_broadcast(P)).then_inc(router_landed, 16)

            def copy_turned(dst, src):
                return nc.scalar.activation(dst.rearrange("p (b k) n -> p b (k n)", b=2), src, ACT.Copy)

            def copy_whole(dst, kind):
                ks = [i for w, i in WHOLE if w == kind] if kind == GU else \
                    [k for w, i in WHOLE if w == kind for k in (2 * i, 2 * i + 1)]
                for k in ks:
                    last = nc.scalar.activation(dst[:, k, :], ps_t[:, k // 4, (k % 4) * P:(k % 4 + 1) * P], ACT.Copy)
                return last

            def high_part(e, unit):
                n = nth(e, unit)
                if not (isinstance(n, int) and n < RING):
                    act.wait_ge(split_used, n + 1 - RING)
                if unit[0] == GU:
                    act.wait_ge(gu_landed[unit[1]], e * 16 + 16)
                else:
                    act.wait_ge(wd_landed[unit[1]], e * 16)
                nc.scalar.activation(high[:, ring_slot(e, unit), :], raw(unit), ACT.Copy).then_inc(high_ready, 1)

            def sigmoid():
                return nc.scalar.activation(sig[:], gate[:], ACT.Sigmoid, scale=SWISH)

            def weigh(g):
                return nc.scalar.activation(y[:].rearrange("p (b n) -> p b n", b=2), ps_y[:], ACT.Copy, scale=g)

            for t in range(NT + 2):
                if t < NT:
                    act.wait_ge(pooled, t + 1)
                    if t >= 2:
                        act.wait_ge(mixed, t - 1)
                    copy_turned(turned[:, t % 2], ps_gu[:, 2 * (t % 2):2 * (t % 2) + 2, :])\
                        .then_inc(pooled_copied, 1)
                if t >= 2:
                    act.wait_ge(var_ready, t - 1)
                    nc.scalar.activation(std[:, t - 2:t - 1], var[:, t - 2:t - 1], ACT.Sqrt).then_inc(std_ready, 1)
                if t == 1:
                    act.wait_ge(bias_step, 5)
                    for s in range(NB):
                        act.dma_start(gub_dram[s].rearrange("e (q n) -> (e q) n", q=4), bpart[:, s, 0:BQ])\
                            .then_inc(bias_stored, 16)
                        act.dma_start(db_dram[s].rearrange("e (q n) -> (e q) n", q=4), bpart[:, s, BQ:])\
                            .then_inc(bias_stored, 16)

            for t in range(NT):
                act.wait_ge(h1_ready, t + 1)
                act.dma_start(h1_dram[t * P:(t + 1) * P, :], h1[:, t, :]).then_inc(h1_stored, 16)
                act.wait_ge(h1_turned, t + 1)
                if t >= 2:
                    act.wait_ge(logits_done, t - 1)
                copy_turned(turned[:, t % 2], ps_gu[:, 2 * (t % 2):2 * (t % 2) + 2, :]).then_inc(h1_copied, 1)
                nc.scalar.activation(z[:, t, :], h1[:, t, :], ACT.Copy, scale=ALPHA).then_inc(h1_scaled, 1)
                act.wait_ge(h1_scaled, t + 1)
                act.dma_start(acc_dram[t * P:(t + 1) * P, :], z[:, t, :]).then_inc(acc_stored, 16)
            act.dma_start(acc_dram[SEQ:SEQ + P, :], z[:, 0, :]).then_inc(acc_stored, 16)

            act.wait_ge(exp_in, 1)
            nc.scalar.activation(gexp[:], gexp[:], ACT.Exp).then_inc(exp_done, 1)

            def iteration(e):
                first, second = isinstance(e, int) and e == 0, isinstance(e, int) and e == 1
                for unit in UNITS:
                    if unit in SPLIT and not (first and unit[0] == DN):
                        high_part(e, unit)
                    if unit == (GU, 2) and not (first or second):
                        act.wait_ge(split_used, nth(e - 1, (DN, KD // 2 - 1)) + 1)
                        act.wait_ge(y_free, e - 1)
                        weigh(slot[:, e - 2:e - 1, 1] if isinstance(e, int) else slot[:, bass.ds(e - 2, 1), 1])\
                            .then_inc(y_ready, 1)
                    if unit == (GU, KD - 1) and not first:
                        act.wait_ge(hid_turned, e)
                        copy_turned(ht_high[:], ps_t[:]).then_inc(ht_high_ready, 1)
                        copy_whole(ht, DN).then_inc(ht_whole_ready, 1)
                    if unit == (DN, 2):
                        act.wait_ge(xg_turned, e + 2)
                        copy_turned(xt_high[:], ps_t[:]).then_inc(xt_high_ready, 1)
                        copy_whole(xt, GU).then_inc(xt_whole_ready, 1)
                act.wait_ge(gate_ready, e + 1)
                sigmoid().then_inc(sig_ready, 1)

            act.wait_ge(h1_stored, 16 * NT)
            act.wait_ge(acc_stored, 16 * (NT + 1))
            act.wait_ge(bias_stored, 32 * NB)
            act.wait_ge(ranked, 1)
            act.wait_ge(xg_turned, 1)
            copy_turned(xt_high[:], ps_t[:]).then_inc(xt_high_ready, 1)
            copy_whole(xt, GU).then_inc(xt_whole_ready, 1)
            iteration(0)
            iteration(1)
            with act.Fori(2, E) as e:
                iteration(e)
            act.wait_ge(split_used, nth(E - 1, (DN, KD // 2 - 1)) + 1)
            act.wait_ge(y_free, E - 1)
            weigh(slot[:, E - 2, 1:2]).then_inc(y_ready, 1)
            act.wait_ge(hid_turned, E)
            copy_turned(ht_high[:], ps_t[:]).then_inc(ht_high_ready, 1)
            copy_whole(ht, DN).then_inc(ht_whole_ready, 1)
            for unit in UNITS[KD:]:
                if unit in SPLIT:
                    high_part(E, unit)
            act.wait_ge(split_used, nth(E, (DN, KD // 2 - 1)) + 1)
            act.wait_ge(y_free, E)
            weigh(slot[:, E - 1, 1:2]).then_inc(y_ready, 1)

            act.wait_ge(most_ready, 1)
            largest = act.value_load(most[0:1, 0:1], min_val=0, max_val=SEQ)
            with act.If(largest > P):
                act.wait_ge(x_tables, 1)
                with act.Fori(0, NX) as n:
                    need = act.value_load(over_i[0:1, bass.ds(n, 1)], min_val=0, max_val=1)
                    with act.If(need > 0):
                        q = act.value_load(seq_i[0:1, bass.ds(n, 1)], min_val=1, max_val=NX)
                        act.wait_ge(x_turned, q)
                        copy_turned(xt[:], ps_t[:]).then_inc(x_xt, 1)
                        act.wait_ge(x_gate, q)
                        sigmoid().then_inc(x_sig, 1)
                        act.wait_ge(x_hturned, q)
                        copy_turned(ht[:], ps_t[:]).then_inc(x_ht, 1)
                        act.wait_ge(x_d, q)
                        weigh(slot_x[:, 1:2]).then_inc(x_y, 1)

            for t in range(NT):
                act.wait_ge(last_var, t + 1)
                nc.scalar.activation(std[:, t:t + 1], var[:, t:t + 1], ACT.Sqrt).then_inc(last_std, 1)

        @block.gpsimd
        def _(pool):
            nc.gpsimd.memset(prev[:], 0.0).then_inc(meta_cleared, 1)
            nc.gpsimd.memset(gu_bias[:], 0.0).then_inc(zeros_set, 1)
            nc.gpsimd.memset(d_bias[:], 0.0).then_inc(zeros_set, 1)
            pool.sem_inc(y_free, 1)

            last_row, last_sum = pool.to_reg(SEQ - 1), pool.to_reg(SEQ + P - 1)

            def gather():
                return nc.gpsimd.indirect_dma_start(
                    out=xg[:], out_offset=None, in_=h1_dram,
                    in_offset=bass.IndirectOffsetOnAxis(ap=gidx[:, 0:1], axis=0),
                    bounds_check=last_row, oob_is_err=False)

            def scatter():
                return nc.gpsimd.indirect_dma_start(
                    out=acc_dram, out_offset=bass.IndirectOffsetOnAxis(ap=sidx[:, 0:1], axis=0),
                    in_=y[:], in_offset=None,
                    bounds_check=last_sum, oob_is_err=True, compute_op=ALU.add)

            pool.wait_ge(wide_landed, 48)
            for t in range(NT):
                pool.wait_ge(gained, t + 1)
                nc.gpsimd.tensor_tensor(h1[:, t, :], h1[:, t, :], wide[:, 2, :], ALU.add).then_inc(h1_ready, 1)

            pool.wait_ge(h1_stored, 16 * NT)
            pool.wait_ge(h1_scaled, NT)
            pool.wait_ge(gidx_ready, 3)
            gather().then_inc(xg_landed, 16)
            pool.wait_ge(gidx_ready, 6)
            pool.wait_ge(xg_turned, 1)
            gather().then_inc(xg_landed, 16)
            pool.wait_ge(gidx_ready, 9)
            pool.wait_ge(xg_turned, 2)
            gather().then_inc(xg_landed, 16)
            with pool.Fori(2, E) as e:
                listed_e1, turned_e, before = pool.to_reg(e * 3 + 6), pool.to_reg(e + 1), pool.to_reg(e - 1)
                added = pool.to_reg((e - 1) * 16)
                pool.wait_ge(h1_stored, 16 * NT)
                pool.wait_ge(gidx_ready, listed_e1)
                pool.wait_ge(xg_turned, turned_e)
                gather().then_inc(xg_landed, 16)
                nc.gpsimd.tensor_copy(sidx[:], sidx_all[:, bass.ds(e - 2, 1)]).then_inc(sidx_ready, 1)
                pool.wait_ge(acc_stored, 16 * (NT + 1))
                pool.wait_ge(sidx_ready, before)
                pool.wait_ge(y_ready, before)
                scatter().then_inc(rows_added, 16)
                pool.wait_ge(rows_added, added)
                pool.sem_inc(y_free, 1)
            for e in (E - 2, E - 1):
                nc.gpsimd.tensor_copy(sidx[:], sidx_all[:, e:e + 1]).then_inc(sidx_ready, 1)
                pool.wait_ge(sidx_ready, e + 1)
                pool.wait_ge(y_ready, e + 1)
                scatter().then_inc(rows_added, 16)
                pool.wait_ge(rows_added, (e + 1) * 16)
                pool.sem_inc(y_free, 1)
            pool.wait_ge(xg_landed, (E + 1) * 16)

            pool.wait_ge(most_ready, 1)
            largest = pool.value_load(most[0:1, 0:1], min_val=0, max_val=SEQ)
            with pool.If(largest > P):
                pool.wait_ge(x_tables, 1)
                pool.sem_inc(x_free, 1)
                with pool.Fori(0, NX) as n:
                    need = pool.value_load(over_i[0:1, bass.ds(n, 1)], min_val=0, max_val=1)
                    with pool.If(need > 0):
                        q = pool.value_load(seq_i[0:1, bass.ds(n, 1)], min_val=1, max_val=NX)
                        listed_q = pool.to_reg(q * 3)
                        pool.wait_ge(h1_stored, 16 * NT)
                        pool.wait_ge(x_gidx, listed_q)
                        gather().then_inc(x_rows, 16)
                        pool.wait_ge(acc_stored, 16 * (NT + 1))
                        pool.wait_ge(x_y, q)
                        scatter().then_inc(x_added, 16)
                        pool.wait_ge(x_added, q * 16)
                        pool.sem_inc(x_free, 1)
            pool.sem_inc(x_end, 1)

            for t in range(NT):
                pool.wait_ge(last_gained, t + 1)
                nc.gpsimd.tensor_tensor(h1[:, t, :], h1[:, t, :], wide[:, 2, :], ALU.add).then_inc(last_ready, 1)

        @block.vector
        def _(dve):
            nc.vector.memset(ones16[:], 1.0).then_inc(small_cast, 1)
            nc.vector.memset(place[:], 0.0).then_inc(small_cast, 1)
            nc.vector.memset(value[:], 0.0).then_inc(small_cast, 1)
            dve.wait_ge(consts_landed, 32)
            nc.vector.tensor_copy(tri16[:], msk[:, M_TRI:M_TRI + P]).then_inc(small_cast, 1)
            nc.vector.tensor_copy(three16[:], msk[:, M_ONE3:M_ONE3 + P]).then_inc(small_cast, 1)
            dve.wait_ge(small_cast, 5)
            nc.vector.tensor_copy(value[:, :, 0:E, 0],
                                  cst[:, C_TOK:C_TOK + NT].unsqueeze(2).to_broadcast([P, NT, E])).then_inc(small_cast, 1)

            dve.wait_ge(biases_landed, 32)
            nc.vector.tensor_copy(bpart[:, 0, :], brow).then_inc(bias_step, 1)
            dve.wait_ge(bias_step, 1)
            nc.vector.tensor_tensor(bres, brow, bpart[:, 0, :], ALU.subtract).then_inc(bias_step, 1)
            dve.wait_ge(bias_step, 2)
            nc.vector.tensor_copy(bpart[:, 1, :], bres).then_inc(bias_step, 1)
            dve.wait_ge(bias_step, 3)
            nc.vector.tensor_tensor(brow, bres, bpart[:, 1, :], ALU.subtract).then_inc(bias_step, 1)
            dve.wait_ge(bias_step, 4)
            nc.vector.tensor_copy(bpart[:, 2, :], brow).then_inc(bias_step, 1)

            def residual(t):
                dve.wait_ge(mixed, t + 1)
                dve.wait_ge(wide_landed, 48)
                src = (ps_y if t % 2 == 0 else ps_t)[:].rearrange("p b n -> p (b n)")
                nc.vector.tensor_tensor(z[:, t, :], src, wide[:, 0, :], ALU.mult).then_inc(mix_evacuated, 1)
                dve.wait_ge(mix_evacuated, t + 1)
                nc.vector.scalar_tensor_tensor(out=z[:, t, :], in0=xin[:, t, :], scalar=ALPHA, in1=z[:, t, :],
                                               op0=ALU.mult, op1=ALU.add).then_inc(ln_step, 1)
                dve.wait_ge(ln_step, 3 * t + 1)
                for b in range(2):
                    nc.vector.bn_stats(stats[:, t, b, :], z[:, t, b * BANK:(b + 1) * BANK]).then_inc(ln_step, 1)
                dve.wait_ge(ln_step, 3 * t + 3)
                nc.vector.bn_aggr(mv[:, t, :], stats[:, t, :, :].rearrange("p b n -> p (b n)")).then_inc(stats_ready, 1)
                dve.wait_ge(stats_ready, t + 1)
                nc.vector.tensor_scalar(var[:, t:t + 1], mv[:, t, 1:2], LN_EPS, None, ALU.add).then_inc(var_ready, 1)

            def inverse_root(t, step):
                r, f = rstd[:, t:t + 1], fix[:, t:t + 1]
                nc.vector.reciprocal(r, std[:, t:t + 1]).then_inc(step, 1)
                dve.wait_ge(step, 4 * t + 1)
                nc.vector.scalar_tensor_tensor(out=f, in0=r, scalar=var[:, t:t + 1], in1=r, op0=ALU.mult,
                                               op1=ALU.mult).then_inc(step, 1)
                dve.wait_ge(step, 4 * t + 2)
                nc.vector.tensor_scalar(f, f, -0.5, 1.5, ALU.mult, ALU.add).then_inc(step, 1)
                dve.wait_ge(step, 4 * t + 3)
                nc.vector.tensor_tensor(r, r, f, ALU.mult).then_inc(step, 1)
                dve.wait_ge(step, 4 * t + 4)

            def normalize(t):
                dve.wait_ge(std_ready, t + 1)
                inverse_root(t, rstd_step)
                nc.vector.tensor_scalar(h1[:, t, :], z[:, t, :], mv[:, t, 0:1], rstd[:, t:t + 1],
                                        ALU.subtract, ALU.mult).then_inc(normed, 1)
                dve.wait_ge(normed, t + 1)
                nc.vector.tensor_tensor(h1[:, t, :], h1[:, t, :], wide[:, 1, :], ALU.mult).then_inc(gained, 1)

            for t in range(NT + 1):
                if t < NT:
                    residual(t)
                if t >= 1:
                    normalize(t - 1)

            dve.wait_ge(router_landed, 32)
            for t in range(NT):
                dve.wait_ge(logits_done, t + 1)
                src = (ps_y if t % 2 == 0 else ps_t)[:, 0, 0:E]
                nc.vector.tensor_tensor(logit[:, t, :], src, rb[:], ALU.add).then_inc(logits_read, 1)
                dve.wait_ge(logits_read, t + 1)
                nc.vector.max(top[:, t, :], logit[:, t, :]).then_inc(route_step, 1)
                dve.wait_ge(route_step, 2 * t + 1)
                nc.vector.max_index(topi[:, t, :], top[:, t, :], logit[:, t, :]).then_inc(route_step, 1)
            rs = 2 * NT

            dve.wait_ge(route_step, rs)
            nc.vector.tensor_tensor(gexp[:], top[:, :, 0:TOPK], top[:, :, 0:1].to_broadcast([P, NT, TOPK]),
                                    ALU.subtract).then_inc(exp_in, 1)
            nc.vector.tensor_copy(topf[:], topi[:]).then_inc(route_step, 1)
            dve.wait_ge(route_step, rs + 1)
            experts = cst[:, C_EXP:C_EXP + E].unsqueeze(1).to_broadcast([P, TOPK, E])
            for t in range(NT):
                nc.vector.tensor_tensor(pick[:, t], topf[:, t, 0:TOPK].unsqueeze(2).to_broadcast([P, TOPK, E]),
                                        experts, ALU.is_equal).then_inc(route_step, 1)
            dve.wait_ge(route_step, rs + 1 + NT)
            nc.vector.tensor_reduce(chosen[:], pick.rearrange("p t k e -> p t e k"), AX.X, ALU.add)\
                .then_inc(route_step, 1)
            dve.wait_ge(route_step, rs + 2 + NT)
            nc.vector.tensor_copy(chosen16[:], chosen[:]).then_inc(chosen_ready, 1)
            dve.wait_ge(exp_done, 1)
            nc.vector.tensor_reduce(gsum[:], gexp[:], AX.X, ALU.add).then_inc(route_step, 1)
            dve.wait_ge(route_step, rs + 3 + NT)
            nc.vector.reciprocal(gsum[:], gsum[:]).then_inc(route_step, 1)
            dve.wait_ge(route_step, rs + 4 + NT)
            nc.vector.tensor_tensor(gates[:], gexp[:], gsum[:].unsqueeze(2).to_broadcast([P, NT, TOPK]), ALU.mult)\
                .then_inc(route_step, 1)
            dve.wait_ge(route_step, rs + 5 + NT)
            for t in range(NT):
                nc.vector.tensor_tensor(pickg[:, t], pick[:, t], gates[:, t].unsqueeze(2).to_broadcast([P, TOPK, E]),
                                        ALU.mult).then_inc(route_step, 1)
            dve.wait_ge(route_step, rs + 5 + 2 * NT)
            dve.wait_ge(small_cast, 6)
            nc.vector.tensor_reduce(value[:, :, 0:E, 1], pickg.rearrange("p t k e -> p t e k"), AX.X, ALU.add)\
                .then_inc(place_ready, 1)
            dve.wait_ge(ranked, 1)
            nc.vector.scalar_tensor_tensor(out=place[:, :, 0:E],
                                           in0=ps_y[:, 1, 0:NT * E].rearrange("p (t e) -> p t e", t=NT), scalar=1.0,
                                           in1=chosen[:], op0=ALU.add, op1=ALU.mult).then_inc(place_ready, 1)
            dve.wait_ge(place_ready, 2)

            def one_hot(at):
                return nc.vector.tensor_tensor(
                    hot[:], at.to_broadcast([P, NT, P]),
                    cst[:, C_SLOT:C_SLOT + P].unsqueeze(1).to_broadcast([P, NT, P]), ALU.is_equal)

            listed = ps_t[:, 0, 0:2]

            def list_part(e):
                if isinstance(e, int):
                    at, what = place[:, :, e:e + 1], value[:, :, e, :]
                else:
                    at = place[:, :, bass.ds(e, 1)]
                    what = value[:, :, bass.ds(e, 1), :].rearrange("p t o c -> p t (o c)")
                one_hot(at).then_inc(hot_step, 1)
                nc.vector.tensor_copy(val[:], what).then_inc(hot_step, 1)

            def read_list(e):
                if isinstance(e, int):
                    slot_e, sidx_e = slot[:, e, :], sidx_all[:, e:e + 1]
                else:
                    slot_e = slot[:, bass.ds(e, 1), :].rearrange("p o c -> p (o c)")
                    sidx_e = sidx_all[:, bass.ds(e, 1)]
                dve.wait_ge(hot_used, e + 1)
                if not (isinstance(e, int) and e == 0):
                    dve.wait_ge(xg_landed, e * 16)
                nc.vector.tensor_copy(slot_e, listed).then_inc(gidx_ready, 1)
                nc.vector.tensor_scalar(sidx_e, listed[:, 0:1], float(ABSENT), cst[:, C_SPARE:C_SPARE + 1],
                                        ALU.add, ALU.min).then_inc(gidx_ready, 1)
                nc.vector.tensor_scalar(gidx[:], listed[:, 0:1], float(ABSENT), None, ALU.add).then_inc(gidx_ready, 1)

            list_part(0)
            read_list(0)

            nc.vector.tensor_copy(count[:], ps_t[0:1, 1, 0:E]).then_inc(route_step, 1)
            dve.wait_ge(route_step, rs + 6 + 2 * NT)
            nc.vector.tensor_reduce(most[:], count[:], AX.X, ALU.max).then_inc(most_ready, 1)

            def clamp_gate():
                return nc.vector.tensor_scalar(gate[:], ps_gu[:, 0:2, :].rearrange("p b n -> p (b n)"), LIMIT, None,
                                               ALU.min)

            def clamp_up():
                return nc.vector.tensor_scalar(up[:], ps_gu[:, 2:4, :].rearrange("p b n -> p (b n)"), LIMIT, -LIMIT,
                                               ALU.min, ALU.max)

            def up_gate():
                return nc.vector.scalar_tensor_tensor(out=up[:], in0=up[:], scalar=1.0, in1=gate[:],
                                                      op0=ALU.add, op1=ALU.mult)

            def hidden():
                return nc.vector.tensor_tensor(up[:], up[:], sig[:], ALU.mult)

            def low_part(e, unit):
                dve.wait_ge(high_ready, nth(e, unit) + 1)
                s = ring_slot(e, unit)
                nc.vector.tensor_tensor(low[:, s, :], raw(unit), high[:, s, :].bitcast(F32), ALU.subtract)\
                    .then_inc(low_ready, 1)

            def low_turned(dst, top_part):
                return nc.vector.tensor_tensor(dst[:].rearrange("p k n -> p (k n)"),
                                               ps_t[:].rearrange("p b n -> p (b n)"),
                                               top_part[:].rearrange("p k n -> p (k n)").bitcast(F32), ALU.subtract)

            def iteration(e):
                first = isinstance(e, int) and e == 0
                for unit in UNITS:
                    if unit in SPLIT and not (first and unit[0] == DN):
                        low_part(e, unit)
                    if unit == (GU, 0):
                        list_part(e + 1)
                    if unit == (GU, 3):
                        read_list(e + 1)
                    if unit == (GU, KD - 1) and not first:
                        dve.wait_ge(ht_high_ready, e)
                        dve.wait_ge(ht_whole_ready, e)
                        low_turned(ht_low, ht_high).then_inc(ht_low_ready, 1)
                    if unit == (DN, 2):
                        dve.wait_ge(xt_high_ready, e + 2)
                        dve.wait_ge(xt_whole_ready, e + 2)
                        low_turned(xt_low, xt_high).then_inc(xt_low_ready, 1)
                        dve.wait_ge(split_used, nth(e, (GU, KD - 1)) + 1)
                        clamp_gate().then_inc(gate_ready, 1)
                        clamp_up().then_inc(up_ready, 1)
                dve.wait_ge(gate_ready, e + 1)
                dve.wait_ge(up_ready, e + 1)
                up_gate().then_inc(act_step, 1)
                dve.wait_ge(act_step, e + 1)
                dve.wait_ge(sig_ready, e + 1)
                hidden().then_inc(hid_ready, 1)

            dve.wait_ge(acc_stored, 16 * (NT + 1))
            dve.wait_ge(h1_stored, 16 * NT)
            dve.wait_ge(xt_high_ready, 1)
            dve.wait_ge(xt_whole_ready, 1)
            low_turned(xt_low, xt_high).then_inc(xt_low_ready, 1)
            iteration(0)
            iteration(1)
            with dve.Fori(2, E) as e:
                iteration(e)
            dve.wait_ge(ht_high_ready, E)
            dve.wait_ge(ht_whole_ready, E)
            low_turned(ht_low, ht_high).then_inc(ht_low_ready, 1)
            for unit in UNITS[KD:]:
                if unit in SPLIT:
                    low_part(E, unit)

            dve.wait_ge(most_ready, 1)
            largest = dve.value_load(most[0:1, 0:1], min_val=0, max_val=SEQ)
            with dve.If(largest > P):
                for j in range(MORE):
                    nc.vector.tensor_scalar(over[:, j * E:(j + 1) * E], count[:], float(P * (j + 1)), None, ALU.is_gt)\
                        .then_inc(x_step, 1)
                    nc.vector.tensor_scalar(place_x[:, :, j * E:(j + 1) * E], place[:, :, 0:E], float(-P * (j + 1)),
                                            None, ALU.add).then_inc(x_step, 1)
                dve.wait_ge(x_step, 2 * MORE)
                nc.vector.tensor_tensor_scan(seq_f[:], over[:], over[:], 0.0, ALU.add, ALU.max).then_inc(x_step, 1)
                nc.vector.tensor_copy(over_i[:], over[:]).then_inc(x_step, 1)
                dve.wait_ge(x_step, 2 * MORE + 2)
                nc.vector.tensor_copy(seq_i[:], seq_f[:]).then_inc(x_tables, 1)
                dve.wait_ge(x_tables, 1)
                for j in range(MORE):
                    with dve.Fori(0, E) as e:
                        need = dve.value_load(over_i[0:1, bass.ds(e + j * E, 1)], min_val=0, max_val=1)
                        with dve.If(need > 0):
                            q = dve.value_load(seq_i[0:1, bass.ds(e + j * E, 1)], min_val=1, max_val=NX)
                            dve.wait_ge(x_free, q)
                            one_hot(place_x[:, :, bass.ds(e + j * E, 1)]).then_inc(x_hot, 1)
                            nc.vector.tensor_copy(
                                val[:], value[:, :, bass.ds(e, 1), :].rearrange("p t o c -> p t (o c)"))\
                                .then_inc(x_hot, 1)
                            dve.wait_ge(x_listed, q)
                            nc.vector.tensor_copy(slot_x[:], listed).then_inc(x_gidx, 1)
                            nc.vector.tensor_scalar(sidx[:], listed[:, 0:1], float(ABSENT),
                                                    cst[:, C_SPARE:C_SPARE + 1], ALU.add, ALU.min).then_inc(x_gidx, 1)
                            nc.vector.tensor_scalar(gidx[:], listed[:, 0:1], float(ABSENT), None, ALU.add)\
                                .then_inc(x_gidx, 1)
                            dve.wait_ge(x_gu, q)
                            clamp_gate().then_inc(x_gate, 1)
                            clamp_up().then_inc(x_up, 1)
                            dve.wait_ge(x_gate, q)
                            dve.wait_ge(x_up, q)
                            up_gate().then_inc(x_upgate, 1)
                            dve.wait_ge(x_upgate, q)
                            dve.wait_ge(x_sig, q)
                            hidden().then_inc(x_hid, 1)

            dve.wait_ge(wide2_landed, 32)
            for t in range(NT + 1):
                if t < NT:
                    dve.wait_ge(sums_landed[t], 16)
                    for b in range(2):
                        nc.vector.bn_stats(stats[:, t, b, :], xin[:, t, b * BANK:(b + 1) * BANK]).then_inc(last_step, 1)
                    dve.wait_ge(last_step, 2 * t + 2)
                    nc.vector.bn_aggr(mv[:, t, :], stats[:, t, :, :].rearrange("p b n -> p (b n)"))\
                        .then_inc(last_stats, 1)
                    dve.wait_ge(last_stats, t + 1)
                    nc.vector.tensor_scalar(var[:, t:t + 1], mv[:, t, 1:2], LN_EPS, None, ALU.add)\
                        .then_inc(last_var, 1)
                if t >= 1:
                    dve.wait_ge(last_std, t)
                    inverse_root(t - 1, last_rstd)
                    nc.vector.tensor_scalar(h1[:, t - 1, :], xin[:, t - 1, :], mv[:, t - 1, 0:1], rstd[:, t - 1:t],
                                            ALU.subtract, ALU.mult).then_inc(last_normed, 1)
                    dve.wait_ge(last_normed, t)
                    nc.vector.tensor_tensor(h1[:, t - 1, :], h1[:, t - 1, :], wide[:, 1, :], ALU.mult)\
                        .then_inc(last_gained, 1)

        @block.tensor
        def _(pe):
            pe.wait_ge(consts_landed, 32)

            def pool_rows(t):
                pe.wait_ge(x_landed[t], 16)
                if t == 0:
                    pe.wait_ge(meta_landed, 16)
                if t >= 2:
                    pe.wait_ge(pooled_copied, t - 1)
                before = prev[:, :] if t == 0 else xin[:, t - 1, :]
                for c in range(KD):
                    dst = ps_gu[:, 2 * (t % 2) + c // 4, (c % 4) * P:(c % 4 + 1) * P]
                    band = msk[:, M_BAND + (c // 2) * 2 * P:M_BAND + (c // 2 + 1) * 2 * P]
                    cols = slice(c * P, (c + 1) * P)
                    nc.tensor.matmul(dst, xin[:, t, cols], band[:, 0:P], start=True, stop=False)
                    last = nc.tensor.matmul(dst, before[:, cols], band[:, P:2 * P], start=False, stop=True)
                last.then_inc(pooled, 1)

            def mix_rows(t):
                pe.wait_ge(pooled_copied, t + 1)
                pe.wait_ge(pw_landed, 16)
                if t >= 2:
                    pe.wait_ge(mix_evacuated, t - 1)
                dst = (ps_y if t % 2 == 0 else ps_t)[:].rearrange("p b n -> p (b n)")
                for g in range(NG):
                    for k in range(2):
                        last = nc.tensor.matmul(dst[:, g * GW:(g + 1) * GW], turned[:, t % 2, 2 * g + k, :],
                                                pw[:, 2 * g + k, :], start=(k == 0), stop=(k == 1))
                last.then_inc(mixed, 1)

            for t in range(NT + 1):
                if t < NT:
                    pool_rows(t)
                if t >= 1:
                    mix_rows(t - 1)

            pe.wait_ge(router_landed, 32)
            for t in range(NT):
                pe.wait_ge(h1_ready, t + 1)
                pe.wait_ge(pooled_copied, NT)
                if t >= 2:
                    pe.wait_ge(h1_copied, t - 1)
                turn(ps_gu[:, 2 * (t % 2):2 * (t % 2) + 2, :], h1[:, t, :]).then_inc(h1_turned, 1)
                pe.wait_ge(h1_copied, t + 1)
                pe.wait_ge(mix_evacuated, NT)
                if t >= 2:
                    pe.wait_ge(logits_read, t - 1)
                dst = (ps_y if t % 2 == 0 else ps_t)[:, 0, 0:E]
                for k in range(KD):
                    last = nc.tensor.matmul(dst, turned[:, t % 2, k, :], rwt[:, k, :], start=(k == 0),
                                            stop=(k == KD - 1))
                last.then_inc(logits_done, 1)

            pe.wait_ge(chosen_ready, 1)
            pe.wait_ge(small_cast, 6)
            rank = ps_y[:, 1, 0:NT * E]
            for t in range(NT):
                dst = rank[:, t * E:(t + 1) * E]
                for s in range(t):
                    nc.tensor.matmul(dst, ones16[:], chosen16[:, s, :], start=(s == 0), stop=False)
                nc.tensor.matmul(dst, tri16[:], chosen16[:, t, :], start=(t == 0), stop=True)
            for t in range(NT):
                last = nc.tensor.matmul(ps_t[:, 1, 0:E], ones16[:], chosen16[:, t, :], start=(t == 0),
                                        stop=(t == NT - 1))
            last.then_inc(ranked, 1)

            listed = ps_t[:, 0, 0:2]
            pe.wait_ge(hot_step, 2)
            pe.wait_ge(logits_read, NT)
            list_slots(listed).then_inc(hot_used, 1)
            pe.wait_ge(xg_landed, 16)
            pe.wait_ge(most_ready, 1)
            turn(ps_t, xg[:]).then_inc(xg_turned, 1)

            def gate_up_unit(e, k):
                if (GU, k) in SPLIT:
                    pe.wait_ge(low_ready, nth(e, (GU, k)) + 1)
                    gate_up_parts(k, ring_slot(e, (GU, k))).then_inc(split_used, 1)
                else:
                    pe.wait_ge(gu_landed[k], e * 16 + 16)
                    gate_up(k).then_inc(whole_used, 1)

            def down_unit(e, j):
                if (DN, j) in SPLIT:
                    pe.wait_ge(low_ready, nth(e, (DN, j)) + 1)
                    down_parts(j, ring_slot(e, (DN, j))).then_inc(split_used, 1)
                else:
                    pe.wait_ge(wd_landed[j], e * 16)
                    down(2 * j)
                    down(2 * j + 1).then_inc(whole_used, 1)

            def iteration(e):
                first = isinstance(e, int) and e == 0
                pe.wait_ge(gub_landed, e * 16 + 16)
                if not first:
                    pe.wait_ge(up_ready, e)
                    pe.wait_ge(gate_ready, e)
                gate_up_bias().then_inc(gub_used, 1)
                pe.wait_ge(xt_low_ready, e + 1)
                pe.wait_ge(xt_whole_ready, e + 1)
                for k in range(KD):
                    gate_up_unit(e, k)
                    if k == 1:
                        pe.wait_ge(hot_step, e * 2 + 4)
                        list_slots(listed).then_inc(hot_used, 1)
                    if k == 4 and not first:
                        pe.wait_ge(hid_ready, e)
                        pe.wait_ge(gidx_ready, e * 3 + 6)
                        turn(ps_t, up[:]).then_inc(hid_turned, 1)
                if not first:
                    pe.wait_ge(ht_low_ready, e)
                    pe.wait_ge(ht_whole_ready, e)
                pe.wait_ge(xg_landed, e * 16 + 32)
                turn(ps_t, xg[:]).then_inc(xg_turned, 1)
                if not first:
                    pe.wait_ge(db_landed, e * 16)
                    if not (isinstance(e, int) and e == 1):
                        pe.wait_ge(y_ready, e - 1)
                    down_bias().then_inc(db_used, 1)
                    for j in range(KD // 2):
                        down_unit(e, j)

            iteration(0)
            iteration(1)
            with pe.Fori(2, E) as e:
                iteration(e)
            pe.wait_ge(hid_ready, E)
            pe.wait_ge(xt_low_ready, E + 1)
            pe.wait_ge(xt_whole_ready, E + 1)
            turn(ps_t, up[:]).then_inc(hid_turned, 1)
            pe.wait_ge(db_landed, E * 16)
            pe.wait_ge(y_ready, E - 1)
            down_bias()
            pe.wait_ge(ht_low_ready, E)
            pe.wait_ge(ht_whole_ready, E)
            for j in range(KD // 2):
                down_unit(E, j)

            largest = pe.value_load(most[0:1, 0:1], min_val=0, max_val=SEQ)
            with pe.If(largest > P):
                pe.wait_ge(x_tables, 1)
                with pe.Fori(0, NX) as n:
                    need = pe.value_load(over_i[0:1, bass.ds(n, 1)], min_val=0, max_val=1)
                    with pe.If(need > 0):
                        q = pe.value_load(seq_i[0:1, bass.ds(n, 1)], min_val=1, max_val=NX)
                        pe.wait_ge(x_hot, q * 2)
                        list_slots(listed).then_inc(x_listed, 1)
                        pe.wait_ge(x_rows, q * 16)
                        turn(ps_t, xg[:]).then_inc(x_turned, 1)
                        pe.wait_ge(x_weights, q * (16 * (KD + 3)))
                        pe.wait_ge(x_xt, q)
                        gate_up_bias()
                        for k in range(KD):
                            last = gate_up(k)
                        last.then_inc(x_gu, 1)
                        pe.wait_ge(x_hid, q)
                        turn(ps_t, up).then_inc(x_hturned, 1)
                        pe.wait_ge(x_ht, q)
                        down_bias()
                        for k in range(KD):
                            last = down(k)
                        last.then_inc(x_d, 1)


_INS = ["x", "meta_tokens", "consts", "masks", "pool_w", "pool_scale", "router_wt", "router_b", "moe_wgu", "moe_bgu",
        "moe_wd", "moe_bd", "ln_g", "ln_b"]


def kernel(**inputs):
    import concourse.bacc as bacc
    from concourse.bass_utils import run_bass_kernel_spmd

    given = {n: np.ascontiguousarray(a) for n, a in inputs.items()}
    given["consts"], given["masks"] = shape_constants()
    given["router_wt"] = np.ascontiguousarray(given["router_w"][0].T)
    given["moe_wgu"] = given["moe_wgu"][0]
    given["moe_wd"] = given["moe_wd"][0]
    nc = bacc.Bacc("TRN2", target_bir_lowering=False, num_devices=1)
    arrays, args = {}, []
    for name in _INS:
        a = given[name]
        arrays[f"in_{name}"] = a
        args.append(nc.dram_tensor(f"in_{name}", a.shape, mybir.dt.from_np(a.dtype), kind="ExternalInput").ap())
    out = nc.dram_tensor("out_rows", (1, SEQ, D), F32, kind="ExternalOutput").ap()
    trunk(nc, *args, out)
    return run_bass_kernel_spmd(nc, [arrays], core_ids=[0]).results[0]["out_rows"]
```

```python
from contextlib import ExitStack

import numpy as np

import concourse.bass as bass
from concourse import mybir

P = 128
SEQ, D, META = 512, 1024, 16
NT = SEQ // P
KD = D // P
WINDOWS = (2, 4, 8, 16)
NG = len(WINDOWS)
HALO = max(WINDOWS)
GW = D // NG
E, TOPK, F = 32, 4, 1024
BANK = 512
NB = 3
ALPHA = 2.0 ** 0.25
LN_EPS = 1e-5
LIMIT, SWISH = 7.0, 1.702
SIZES = range(40, 100, 4)
BQ = 2 * F // 4
ABSENT = 4096
MORE = SEQ // P - 1
NX = MORE * E

F32, F32R, BF16 = mybir.dt.float32, mybir.dt.float32r, mybir.dt.bfloat16
I32, U32 = mybir.dt.int32, mybir.dt.uint32
ALU, ACT, AX = mybir.AluOpType, mybir.ActivationFunctionType, mybir.AxisListType

GU, DN = 0, 1
UNITS = [(GU, k) for k in range(KD)] + [(DN, j) for j in range(KD // 2)]
NU = len(UNITS)
RING = 3
DEPTH = 3
WARM, WARM_AGAIN = 12, 9
UW = 2 * F
assert NU % RING == 0


def nth(e, unit):
    i = UNITS.index(unit)
    if isinstance(e, int) and e == 0:
        return i
    if isinstance(e, int) and e == E:
        return NU * (E - 1) + i
    return e * NU + (KD - NU + i)


def ring_slot(e, unit):
    if isinstance(e, int) and e in (0, E):
        return nth(e, unit) % RING
    return (KD + UNITS.index(unit)) % RING


def done_before(e):
    if isinstance(e, int) and e == 0:
        return UNITS[:RING] + UNITS[KD:]
    if isinstance(e, int) and e == 1:
        return UNITS[:2]
    return []


C_ID = 0
C_SLOT = C_ID + P
C_EXP = C_SLOT + P
C_TOK = C_EXP + E
C_SPARE = C_TOK + NT
C_ALL = C_SPARE + 1
M_OWN = 0
M_BEFORE = M_OWN + NG * P
M_TRI = M_BEFORE + NG * NT * HALO
M_ONE3 = M_TRI + P
M_ALL = M_ONE3 + P


def shape_constants():
    c, m = np.zeros((P, C_ALL), np.float32), np.zeros((P, M_ALL), np.float32)
    i = np.arange(P)
    s, t = i[:, None], i[None, :]
    c[:, C_ID:C_ID + P] = np.eye(P)
    c[:, C_SLOT:C_SLOT + P] = i + 1
    c[:, C_EXP:C_EXP + E] = np.arange(E)
    c[:, C_TOK:C_TOK + NT] = i[:, None] + P * np.arange(NT) - ABSENT
    c[:, C_SPARE] = SEQ + i
    for g, win in enumerate(WINDOWS):
        m[:, M_OWN + g * P:M_OWN + (g + 1) * P] = ((s <= t) & (s > t - win)) / win - (s == t)
        at = M_BEFORE + g * NT * HALO
        for n in range(NT):
            m[n * HALO:(n + 1) * HALO, at + n * HALO:at + (n + 1) * HALO] = \
                (s[0:HALO] - HALO > t[:, 0:HALO] - win) / win
    m[:, M_TRI:M_TRI + P] = s < t
    m[:NB, M_ONE3:M_ONE3 + P] = 1
    return c, m


def trunk(nc, x, meta, consts, masks, pool_w, pool_scale, router_wt, router_b, wgu, bgu, wd, bd, ln_g, ln_b, out):
    ctx = ExitStack()
    with ctx:
        def sb(name, shape, dt=F32):
            return ctx.enter_context(nc.sbuf_tensor(name, shape, dt))

        def sem(name):
            return ctx.enter_context(nc.semaphore(name))

        h1_dram = nc.dram_tensor("h1_rows", [SEQ, D], F32, kind="Internal").ap()
        acc_dram = nc.dram_tensor("acc_rows", [SEQ + P, D], F32, kind="Internal").ap()
        gub_dram = nc.dram_tensor("gu_bias_parts", [NB, E, 2 * F], BF16, kind="Internal").ap()
        db_dram = nc.dram_tensor("d_bias_parts", [NB, E, D], BF16, kind="Internal").ap()

        cst = sb("cst", [P, C_ALL])
        gu_ring = sb("gu_ring", [P, KD, 2 * F])
        wd_ring = sb("wd_ring", [P, KD, D])
        rb = sb("rb", [P, E])
        stats = sb("stats", [P, NT, 2, 6])
        mv = sb("mv", [P, NT, 2])
        var = sb("var", [P, NT])
        std = sb("std", [P, NT])
        rstd = sb("rstd", [P, NT])
        fix = sb("fix", [P, NT])
        logit = sb("logit", [P, NT, E])
        top = sb("top", [P, NT, 8])
        topi = sb("topi", [P, NT, 8], U32)
        topf = sb("topf", [P, NT, 8])
        gexp = sb("gexp", [P, NT, E])
        gsum = sb("gsum", [P, NT])
        chosen = sb("chosen", [P, NT, E])
        chosen16 = sb("chosen16", [P, NT, E], BF16)
        place = sb("place", [P, NT, E])
        value = sb("value", [P, NT, E, 2])
        tri16 = sb("tri16", [P, P], BF16)
        ones16 = sb("ones16", [P, P], BF16)
        three16 = sb("three16", [P, P], BF16)
        count = sb("count", [1, E])
        tally = sb("tally", [1, E], I32)
        most = sb("most", [1, 1], I32)
        hot = sb("hot", [P, NT, P])
        pick = hot[:].rearrange("p t (k e) -> p t k e", k=TOPK)
        val = sb("val", [P, NT, 2])
        slot = sb("slot", [P, E, 2])
        gidx = sb("gidx", [P, 1], I32)
        sidx_all = sb("sidx_all", [P, E], I32)
        sidx = sb("sidx", [P, 1], I32)
        gu_bias = sb("gu_bias", [P, 2 * F], BF16)
        d_bias = sb("d_bias", [P, D], BF16)
        place_x = sb("place_x", [P, NT, NX])
        over = sb("over", [1, NX])
        seq_f = sb("seq_f", [1, NX])
        over_i = sb("over_i", [1, NX], I32)
        seq_i = sb("seq_i", [1, NX], I32)
        slot_x = sb("slot_x", [P, 2])

        with ExitStack() as early:
            def sb_early(name, shape, dt=F32):
                return early.enter_context(nc.sbuf_tensor(name, shape, dt))

            xin = sb_early("xin", [P, NT, D])
            wide = sb_early("wide", [P, 3, D])
            halo = sb_early("halo", [NT * HALO, D])
            pw = sb_early("pw", [P, NG * 2, GW])
            msk = sb_early("msk", [P, M_ALL])
            bpart = sb_early("bpart", [P, NB, BQ + D // 4], BF16)
            brow = sb_early("brow", [P, BQ + D // 4])
            turned = sb_early("turned", [P, 2, KD, P])
            rwt = sb_early("rwt", [P, KD, E])
            z = sb_early("z", [P, NT, D])
            h1 = sb_early("h1", [P, NT, D])
        bres = z[:, 3, 0:BQ + D // 4]
        halo_t = h1[:, NT - 1, 0:KD * NT * HALO].rearrange("p (k n) -> p k n", k=KD)
        gain2 = pw[:, 0:NG, :].rearrange("p g n -> p (g n)")
        bias2 = pw[:, NG:, :].rearrange("p g n -> p (g n)")

        high = sb("high", [P, RING, UW], F32R)
        low = sb("low", [P, RING, UW], F32R)
        xt_high = sb("xt_high", [P, KD, P], F32R)
        xt_low = sb("xt_low", [P, KD, P], F32R)
        ht_high = sb("ht_high", [P, KD, P], F32R)
        ht_low = sb("ht_low", [P, KD, P], F32R)
        xt = sb("xt", [P, KD, P])
        ht = sb("ht", [P, KD, P])
        gate = sb("gate", [P, F])
        sig = sb("sig", [P, F])
        up = sb("up", [P, F])
        xg = sb("xg", [P, D])
        y = sb("y", [P, D])

        ident = cst[:, C_ID:C_ID + P]

        ps_gu = ctx.enter_context(nc.psum_tensor("ps_gu", [P, 4, BANK], F32))
        ps_y = ctx.enter_context(nc.psum_tensor("ps_y", [P, 2, BANK], F32))
        ps_t = ctx.enter_context(nc.psum_tensor("ps_t", [P, 2, BANK], F32))

        x_landed = [sem(f"x_landed{t}") for t in range(NT)]
        masks_landed = sem("masks_landed")
        consts_landed = sem("consts_landed")
        halo_landed = sem("halo_landed")
        halo_pooled = sem("halo_pooled")
        halo_copied = sem("halo_copied")
        pw_landed = sem("pw_landed")
        scale_landed = sem("scale_landed")
        wide_landed = sem("wide_landed")
        spread_done = sem("spread_done")
        wide_ready = sem("wide_ready")
        pw_scaled = sem("pw_scaled")
        router_landed = sem("router_landed")
        biases_landed = sem("biases_landed")
        pooled = sem("pooled")
        pooled_copied = sem("pooled_copied")
        pooled_whole = sem("pooled_whole")
        mixed = sem("mixed")
        mix_evacuated = sem("mix_evacuated")
        ln_step = sem("ln_step")
        stats_ready = sem("stats_ready")
        var_ready = sem("var_ready")
        std_ready = sem("std_ready")
        rstd_step = sem("rstd_step")
        centred = sem("centred")
        scaled = sem("scaled")
        h1_ready = sem("h1_ready")
        h1_scaled = sem("h1_scaled")
        h1_stored = sem("h1_stored")
        acc_stored = sem("acc_stored")
        h1_turned = sem("h1_turned")
        h1_copied = sem("h1_copied")
        logits_done = sem("logits_done")
        logits_read = sem("logits_read")
        bias_step = sem("bias_step")
        bias_stored = sem("bias_stored")
        zeros_set = sem("zeros_set")
        small_cast = sem("small_cast")
        route_step = sem("route_step")
        exp_in = sem("exp_in")
        exp_done = sem("exp_done")
        chosen_step = sem("chosen_step")
        chosen_ready = sem("chosen_ready")
        ranked = sem("ranked")
        place_ready = sem("place_ready")
        most_ready = sem("most_ready")
        gu_landed = [sem(f"gu_landed{k}") for k in range(KD)]
        wd_landed = [sem(f"wd_landed{k}") for k in range(KD // 2)]
        high_ready = sem("high_ready")
        low_ready = sem("low_ready")
        split_used = sem("split_used")
        gub_landed = sem("gub_landed")
        gub_used = sem("gub_used")
        db_landed = sem("db_landed")
        db_used = sem("db_used")
        hot_step = sem("hot_step")
        hot_used = sem("hot_used")
        gidx_ready = sem("gidx_ready")
        xg_landed = sem("xg_landed")
        xg_turned = sem("xg_turned")
        xt_high_ready = sem("xt_high_ready")
        xt_low_ready = sem("xt_low_ready")
        act_step = sem("act_step")
        gate_ready = sem("gate_ready")
        up_ready = sem("up_ready")
        y_free = sem("y_free")
        sig_ready = sem("sig_ready")
        hid_ready = sem("hid_ready")
        hid_turned = sem("hid_turned")
        ht_high_ready = sem("ht_high_ready")
        ht_low_ready = sem("ht_low_ready")
        y_ready = sem("y_ready")
        sidx_ready = sem("sidx_ready")
        rows_added = sem("rows_added")
        x_tables = sem("x_tables")
        x_step = sem("x_step")
        x_free = sem("x_free")
        x_weights = sem("x_weights")
        x_hot = sem("x_hot")
        x_listed = sem("x_listed")
        x_gidx = sem("x_gidx")
        x_rows = sem("x_rows")
        x_turned = sem("x_turned")
        x_xt = sem("x_xt")
        x_gu = sem("x_gu")
        x_gate = sem("x_gate")
        x_up = sem("x_up")
        x_upgate = sem("x_upgate")
        x_sig = sem("x_sig")
        x_hid = sem("x_hid")
        x_hturned = sem("x_hturned")
        x_ht = sem("x_ht")
        x_d = sem("x_d")
        x_y = sem("x_y")
        x_added = sem("x_added")
        x_end = sem("x_end")
        wide2_landed = sem("wide2_landed")
        sums_landed = [sem(f"sums_landed{t}") for t in range(NT)]
        table_loaded = sem("table_loaded")
        last_step = sem("last_step")
        last_stats = sem("last_stats")
        last_var = sem("last_var")
        last_std = sem("last_std")
        last_rstd = sem("last_rstd")
        last_square = sem("last_square")
        last_centred = sem("last_centred")
        last_scaled = sem("last_scaled")
        last_ready = [sem(f"last_ready{t}") for t in range(NT)]
        out_stored = sem("out_stored")

        wgu_v = wgu.rearrange("e (k p) n -> e p k n", p=P)
        wd_v = wd.rearrange("e (k p) n -> e p k n", p=P)

        def turn(dst, src):
            for k in range(KD):
                last = nc.tensor.transpose(dst[:, k // 4, (k % 4) * P:(k % 4 + 1) * P],
                                           src[:, k * P:(k + 1) * P], ident)
            return last

        def gate_up_bias():
            for n in range(4):
                last = nc.tensor.matmul(ps_gu[:, n, :], three16[:], gu_bias[:, n * BANK:(n + 1) * BANK],
                                        start=True, stop=False)
            return last

        def gate_up(k):
            for n in range(4):
                last = nc.tensor.matmul(ps_gu[:, n, :], xt[:, k, :], gu_ring[:, k, n * BANK:(n + 1) * BANK],
                                        start=False, stop=(k == KD - 1))
            return last

        def gate_up_parts(k, s):
            for n in range(4):
                cols = slice(n * BANK, (n + 1) * BANK)
                nc.tensor.matmul(ps_gu[:, n, :], xt_high[:, k, :], high[:, s, cols], start=False, stop=False)
                nc.tensor.matmul(ps_gu[:, n, :], xt_high[:, k, :], low[:, s, cols], start=False, stop=False)
            for n in range(4):
                last = nc.tensor.matmul(ps_gu[:, n, :], xt_low[:, k, :], high[:, s, n * BANK:(n + 1) * BANK],
                                        start=False, stop=(k == KD - 1))
            return last

        def down_bias(dst=ps_y):
            for n in range(2):
                last = nc.tensor.matmul(dst[:, n, :], three16[:], d_bias[:, n * BANK:(n + 1) * BANK],
                                        start=True, stop=False)
            return last

        def down(k):
            for n in range(2):
                last = nc.tensor.matmul(ps_y[:, n, :], ht[:, k, :], wd_ring[:, k, n * BANK:(n + 1) * BANK],
                                        start=False, stop=(k == KD - 1))
            return last

        def down_parts(j, s, dst, hid_high, hid_low):
            for k in (2 * j, 2 * j + 1):
                for n in range(2):
                    at = (k % 2) * D + n * BANK
                    nc.tensor.matmul(dst[:, n, :], hid_high[:, k, :], high[:, s, at:at + BANK],
                                     start=False, stop=False)
                    nc.tensor.matmul(dst[:, n, :], hid_high[:, k, :], low[:, s, at:at + BANK],
                                     start=False, stop=False)
                for n in range(2):
                    at = (k % 2) * D + n * BANK
                    last = nc.tensor.matmul(dst[:, n, :], hid_low[:, k, :], high[:, s, at:at + BANK],
                                            start=False, stop=(k == KD - 1))
            return last

        def raw(e, unit):
            kind, i = unit
            if kind == GU or (isinstance(e, int) and e == E):
                return gu_ring[:, i, :]
            return wd_ring[:, 2 * i:2 * i + 2, :].rearrange("p k n -> p (k n)")

        def list_slots(bank):
            for t in range(NT):
                last = nc.tensor.matmul(bank, hot[:, t, :], val[:, t, :], start=(t == 0), stop=(t == NT - 1))
            return last

        block = ctx.enter_context(nc.Block())

        @block.sync
        def _(sp):
            sp.dma_start(halo[0:META, :], meta).then_inc(halo_landed, 16)
            for t in range(1, NT):
                sp.dma_start(halo[t * HALO:(t + 1) * HALO, :], x[0, t * P - HALO:t * P, :]).then_inc(halo_landed, 16)
            for t in range(NT):
                sp.dma_start(xin[:, t, :], x[0, t * P:(t + 1) * P, :]).then_inc(x_landed[t], 16)
                if t == 0:
                    sp.dma_start(pw[:], pool_w[0].rearrange("g (k p) n -> p (g k) n", p=P)).then_inc(pw_landed, 16)

            def load_gu(e, k):
                sp.dma_start(gu_ring[:, k, :], wgu_v[e, :, k, :]).then_inc(gu_landed[k], 16)

            def load_wd(e, k2):
                sp.dma_start(wd_ring[:, 2 * k2:2 * k2 + 2, :], wd_v[e, :, 2 * k2:2 * k2 + 2, :])\
                    .then_inc(wd_landed[k2], 16)

            def load_gu_bias(e):
                sp.dma_start(gu_bias[0:NB, :], gub_dram[:, e, :]).then_inc(gub_landed, 16)

            def load_d_bias(e):
                sp.dma_start(d_bias[0:NB, :], db_dram[:, e, :]).then_inc(db_landed, 16)

            def reuse(e, unit):
                sp.wait_ge(low_ready, nth(e, unit) + 1)

            for k in range(KD):
                load_gu(0, k)
            for t in range(NT):
                sp.wait_ge(h1_ready, t + 1)
                sp.dma_start(h1_dram[t * P:(t + 1) * P, :], h1[:, t, :]).then_inc(h1_stored, 16)
                if t == 1:
                    sp.wait_ge(bias_stored, 32 * NB)
                    sp.wait_ge(zeros_set, 2)
                    load_gu_bias(0)
                    load_d_bias(0)
                if t >= 1:
                    load_wd(0, t - 1)
            load_wd(0, KD // 2 - 1)
            for k in range(KD):
                if k == 1:
                    sp.wait_ge(xg_landed, 16)
                if k == RING:
                    sp.wait_ge(gub_used, 1)
                    load_gu_bias(1)
                reuse(0, (GU, k))
                load_gu(1, k)

            def landed_counts(e):
                counts = (e + 1) * 16, e * 16, (e - 1) * 16
                return counts if isinstance(e, int) else tuple(sp.to_reg(c) for c in counts)

            def in_turn(unit, gu_count, wd_count, wd_before):
                back = UNITS.index(unit) - DEPTH
                kind, i = UNITS[back]
                if back < 0:
                    sp.wait_ge(wd_landed[i], wd_before)
                elif kind == GU:
                    sp.wait_ge(gu_landed[i], gu_count)
                else:
                    sp.wait_ge(wd_landed[i], wd_count)

            def ahead(e):
                counts = landed_counts(e)
                for k in range(KD):
                    if k == RING:
                        sp.wait_ge(gub_used, e)
                        load_gu_bias(e)
                    reuse(e - 1, (GU, k))
                    in_turn((GU, k), *counts)
                    load_gu(e, k)
                for j in range(KD // 2):
                    if j == RING:
                        sp.wait_ge(db_used, e - 1)
                        load_d_bias(e - 1)
                    reuse(e - 1, (DN, j))
                    in_turn((DN, j), *counts)
                    load_wd(e - 1, j)

            ahead(2)
            with sp.Fori(3, E) as e:
                ahead(e)
            for j in range(KD // 2):
                if j == RING:
                    sp.wait_ge(db_used, E - 1)
                    load_d_bias(E - 1)
                reuse(E - 1, (GU, j))
                if j < DEPTH:
                    sp.wait_ge(wd_landed[KD // 2 - DEPTH + j], (E - 1) * 16)
                else:
                    sp.wait_ge(gu_landed[j - DEPTH], (E + 1) * 16)
                sp.dma_start(gu_ring[:, j, :].rearrange("p (k n) -> p k n", k=2), wd_v[E - 1, :, 2 * j:2 * j + 2, :])\
                    .then_inc(gu_landed[j], 16)

            sp.wait_ge(split_used, nth(E, (DN, KD // 2 - 2)) + 1)
            sp.dma_start(gain2, ln_g[0, 1].partition_broadcast(P)).then_inc(wide2_landed, 16)
            sp.dma_start(bias2, ln_b[0, 1].partition_broadcast(P)).then_inc(wide2_landed, 16)

            sp.wait_ge(most_ready, 2)
            largest = sp.value_load(most[0:1, 0:1], min_val=0, max_val=SEQ)
            with sp.If(largest > P):
                sp.wait_ge(x_tables, 1)
                for j in range(MORE):
                    with sp.Fori(0, E) as e:
                        need = sp.value_load(over_i[0:1, bass.ds(e + j * E, 1)], min_val=0, max_val=1)
                        with sp.If(need > 0):
                            q = sp.value_load(seq_i[0:1, bass.ds(e + j * E, 1)], min_val=1, max_val=NX)
                            sp.wait_ge(x_free, q)
                            sp.dma_start(gu_bias[0:NB, :], gub_dram[:, e, :]).then_inc(x_weights, 16)
                            sp.dma_start(d_bias[0:NB, :], db_dram[:, e, :]).then_inc(x_weights, 16)
                            for k in range(KD):
                                sp.dma_start(gu_ring[:, k, :], wgu_v[e, :, k, :]).then_inc(x_weights, 16)
                            sp.dma_start(wd_ring[:], wd_v[e]).then_inc(x_weights, 16)
                sp.wait_ge(x_end, 1)

            sp.wait_ge(rows_added, 16 * E)
            for t in range(NT):
                sp.dma_start(xin[:, t, :], acc_dram[t * P:(t + 1) * P, :]).then_inc(sums_landed[t], 16)
            for t in (*range(NT - 2), NT - 1, NT - 2):
                sp.wait_ge(last_ready[t], 1)
                sp.dma_start(out[0, t * P:(t + 1) * P, :], h1[:, t, :]).then_inc(out_stored, 16)
            sp.wait_ge(out_stored, 16 * NT)

        @block.scalar
        def _(act):
            act.dma_start(msk[:], masks).then_inc(masks_landed, 16)
            act.dma_start(wide[0:1, 0, :], pool_scale).then_inc(scale_landed, 16)
            act.dma_start(brow[:, 0:BQ], bgu[0].rearrange("e (q n) -> (e q) n", q=4)).then_inc(biases_landed, 16)
            act.dma_start(brow[:, BQ:], bd[0].rearrange("e (q n) -> (e q) n", q=4)).then_inc(biases_landed, 16)
            act.dma_start(wide[0:1, 1, :], ln_g[0, 0:1]).then_inc(wide_landed, 16)
            act.dma_start(wide[0:1, 2, :], ln_b[0, 0:1]).then_inc(wide_landed, 16)
            act.dma_start(cst[:], consts).then_inc(consts_landed, 16)
            act.dma_start(rwt[:], router_wt.rearrange("(k p) e -> p k e", p=P)).then_inc(router_landed, 16)
            act.dma_start(rb[:], router_b[0].partition_broadcast(P)).then_inc(router_landed, 16)

            def copy_turned(dst, src):
                return nc.scalar.activation(dst.rearrange("p (b k) n -> p b (k n)", b=2), src, ACT.Copy)

            def high_part(e, unit):
                n = nth(e, unit)
                if not (isinstance(n, int) and n < RING):
                    act.wait_ge(split_used, n + 1 - RING)
                if unit[0] == GU or (isinstance(e, int) and e == E):
                    act.wait_ge(gu_landed[unit[1]], e * 16 + 16)
                else:
                    act.wait_ge(wd_landed[unit[1]], e * 16)
                nc.scalar.activation(high[:, ring_slot(e, unit), :], raw(e, unit), ACT.Copy).then_inc(high_ready, 1)

            def sigmoid():
                return nc.scalar.activation(sig[:], gate[:], ACT.Sigmoid, scale=SWISH)

            def weigh(g, src=ps_y[:]):
                return nc.scalar.activation(y[:].rearrange("p (b n) -> p b n", b=2), src, ACT.Copy, scale=g)

            def pooled_out(t):
                act.wait_ge(pooled, t + 1)
                if t >= 2:
                    act.wait_ge(mixed, t - 1)
                copy_turned(turned[:, t % 2], ps_gu[:, 2 * (t % 2):2 * (t % 2) + 2, :]).then_inc(pooled_copied, 1)

            def root(t):
                act.wait_ge(var_ready, t + 1)
                nc.scalar.activation(std[:, t:t + 1], var[:, t:t + 1], ACT.Sqrt).then_inc(std_ready, 1)

            def scale_rows(t):
                act.wait_ge(centred, t + 1)
                act.wait_ge(rstd_step, 4 * t + 4)
                nc.scalar.activation(h1[:, t, :], h1[:, t, :], ACT.Copy, scale=rstd[:, t:t + 1]).then_inc(scaled, 1)

            def h1_out(t):
                act.wait_ge(h1_turned, t + 1)
                if t == 0:
                    act.wait_ge(mixed, NT)
                if t >= 2:
                    act.wait_ge(logits_done, t - 1)
                copy_turned(turned[:, t % 2], ps_gu[:, 2 * (t % 2):2 * (t % 2) + 2, :]).then_inc(h1_copied, 1)

            def start_sum(t):
                nc.scalar.activation(z[:, t, :], h1[:, t, :], ACT.Copy, scale=ALPHA).then_inc(h1_scaled, 1)

            def store_sum(t):
                act.dma_start(acc_dram[t * P:(t + 1) * P, :], z[:, t, :]).then_inc(acc_stored, 16)

            def wide_out(v):
                act.wait_ge(spread_done, v + 1)
                nc.scalar.activation(wide[:, v, :].rearrange("p (b n) -> p b n", b=2), (ps_y if v == 0 else ps_t)[:],
                                     ACT.Copy).then_inc(wide_ready, 1)

            act.wait_ge(halo_pooled, 1)
            nc.scalar.activation(halo_t, ps_t[:, 0, :].rearrange("p (k n) -> p k n", k=KD), ACT.Copy)\
                .then_inc(halo_copied, 1)
            wide_out(0)
            pooled_out(0)
            pooled_out(1)
            wide_out(1)
            wide_out(2)
            act.wait_ge(bias_step, 5)
            for s in range(NB):
                act.dma_start(gub_dram[s].rearrange("e (q n) -> (e q) n", q=4), bpart[:, s, 0:BQ])\
                    .then_inc(bias_stored, 16)
                act.dma_start(db_dram[s].rearrange("e (q n) -> (e q) n", q=4), bpart[:, s, BQ:])\
                    .then_inc(bias_stored, 16)
            pooled_out(2)
            root(0)
            scale_rows(0)
            pooled_out(3)
            root(1)
            scale_rows(1)
            root(2)
            h1_out(0)
            root(3)
            h1_out(1)
            h1_out(2)
            act.wait_ge(h1_ready, 2)
            start_sum(0)
            start_sum(1)
            h1_out(3)
            act.wait_ge(h1_ready, NT)
            start_sum(2)
            start_sum(3)
            act.wait_ge(h1_scaled, NT)
            store_sum(0)
            act.wait_ge(exp_in, NT)
            nc.scalar.activation(gexp[:], gexp[:], ACT.Exp).then_inc(exp_done, 1)

            def iteration(e):
                first, second, last = (isinstance(e, int) and e == n for n in (0, 1, E - 1))
                for unit in UNITS:
                    if unit not in done_before(e):
                        high_part(e, unit)
                    if first and unit in ((DN, 0), (DN, 1)):
                        high_part(1, (GU, unit[1]))
                    if unit == (GU, 2) and not (first or second):
                        act.wait_ge(split_used, nth(e - 1, (DN, KD // 2 - 1)) + 1)
                        act.wait_ge(y_free, e - 1)
                        weigh(slot[:, e - 2:e - 1, 1] if isinstance(e, int) else slot[:, bass.ds(e - 2, 1), 1])\
                            .then_inc(y_ready, 1)
                    if unit == (GU, 0) and not first:
                        if second:
                            act.wait_ge(acc_stored, 16 * (NT + 1))
                        act.wait_ge(gate_ready, e)
                        sigmoid().then_inc(sig_ready, 1)
                    if unit == (DN, 0) and not first:
                        act.wait_ge(hid_turned, e)
                        copy_turned(ht_high[:], ps_t[:]).then_inc(ht_high_ready, 1)
                    if unit == (DN, 3) and not last:
                        act.wait_ge(xg_turned, e + 2)
                        copy_turned(xt_high[:], ps_t[:]).then_inc(xt_high_ready, 1)
                    if unit == (DN, 2) and last:
                        act.wait_ge(gate_ready, E)
                        sigmoid().then_inc(sig_ready, 1)

            act.wait_ge(bias_stored, 32 * NB)
            act.wait_ge(small_cast, 6)
            for k in range(RING):
                high_part(0, (GU, k))
            act.wait_ge(h1_stored, 16 * NT)
            act.wait_ge(ranked, 1)
            act.wait_ge(xg_turned, 1)
            copy_turned(xt_high[:], ps_t[:]).then_inc(xt_high_ready, 1)
            for t in range(1, NT):
                store_sum(t)
            act.dma_start(acc_dram[SEQ:SEQ + P, :], z[:, 0, :]).then_inc(acc_stored, 16)
            iteration(0)
            iteration(1)
            with act.Fori(2, E - 1) as e:
                iteration(e)
            iteration(E - 1)
            high_part(E, (DN, 0))
            act.wait_ge(hid_turned, E)
            copy_turned(xt_high[:], ps_t[:]).then_inc(ht_high_ready, 1)
            high_part(E, (DN, 1))
            act.wait_ge(split_used, nth(E - 1, (DN, KD // 2 - 1)) + 1)
            act.wait_ge(y_free, E - 1)
            weigh(slot[:, E - 2, 1:2]).then_inc(y_ready, 1)
            for unit in UNITS[KD + 2:]:
                high_part(E, unit)
            act.wait_ge(split_used, nth(E, (DN, KD // 2 - 1)) + 1)
            act.wait_ge(y_free, E)
            weigh(slot[:, E - 1, 1:2], ps_gu[:, 0:2, :]).then_inc(y_ready, 1)

            act.wait_ge(most_ready, 2)
            largest = act.value_load(most[0:1, 0:1], min_val=0, max_val=SEQ)
            with act.If(largest > P):
                act.wait_ge(x_tables, 1)
                with act.Fori(0, NX) as n:
                    need = act.value_load(over_i[0:1, bass.ds(n, 1)], min_val=0, max_val=1)
                    with act.If(need > 0):
                        q = act.value_load(seq_i[0:1, bass.ds(n, 1)], min_val=1, max_val=NX)
                        act.wait_ge(x_turned, q)
                        copy_turned(xt[:], ps_t[:]).then_inc(x_xt, 1)
                        act.wait_ge(x_gate, q)
                        sigmoid().then_inc(x_sig, 1)
                        act.wait_ge(x_hturned, q)
                        copy_turned(ht[:], ps_t[:]).then_inc(x_ht, 1)
                        act.wait_ge(x_d, q)
                        weigh(slot_x[:, 1:2]).then_inc(x_y, 1)

            nc.scalar.activation(std[:, 0:1], cst[:, C_ID:C_ID + 1], ACT.Sqrt).then_inc(table_loaded, 1)
            act.wait_ge(table_loaded, 1)
            for t in range(NT):
                if t % 2 == 0:
                    act.wait_ge(last_var, t // 2 + 1)
                    nc.scalar.activation(std[:, t:t + 2], var[:, t:t + 2], ACT.Sqrt).then_inc(last_std, 1)
                if t < NT - 1:
                    act.wait_ge(last_centred, t + 1)
                    act.wait_ge(last_rstd, 4 * (t // 2) + 4)
                    nc.scalar.activation(h1[:, t, :], h1[:, t, :], ACT.Copy, scale=rstd[:, t:t + 1])\
                        .then_inc(last_scaled, 1)

        @block.gpsimd
        def _(pool):
            nc.gpsimd.memset(d_bias[:], 0.0).then_inc(zeros_set, 1)
            nc.gpsimd.memset(gu_bias[:], 0.0).then_inc(zeros_set, 1)
            pool.sem_inc(y_free, 1)

            last_row, last_sum = pool.to_reg(SEQ - 1), pool.to_reg(SEQ + P - 1)

            def gather(rows=P):
                return nc.gpsimd.indirect_dma_start(
                    out=xg[0:rows, :], out_offset=None, in_=h1_dram,
                    in_offset=bass.IndirectOffsetOnAxis(ap=gidx[0:rows, 0:1], axis=0),
                    bounds_check=last_row, oob_is_err=False)

            def scatter(rows=P):
                return nc.gpsimd.indirect_dma_start(
                    out=acc_dram, out_offset=bass.IndirectOffsetOnAxis(ap=sidx[0:rows, 0:1], axis=0),
                    in_=y[0:rows, :], in_offset=None,
                    bounds_check=last_sum, oob_is_err=True, compute_op=ALU.add)

            def tokens_of(e):
                return pool.value_load(tally[0:1, bass.ds(e, 1)], min_val=0, max_val=SEQ)

            def sized(move, tokens, signal):
                def least(sizes, rows):
                    if not sizes:
                        move(rows).then_inc(signal, 16)
                        return
                    half = len(sizes) // 2
                    with pool.If(tokens > sizes[half]):
                        least(sizes[half + 1:], rows)
                    with pool.Else():
                        least(sizes[:half], sizes[half])

                least(SIZES, P)

            pool.wait_ge(wide_ready, 3)
            for t in range(NT // 2):
                pool.wait_ge(scaled, t + 1)
                nc.gpsimd.tensor_tensor(h1[:, t, :], h1[:, t, :], wide[:, 2, :], ALU.add).then_inc(h1_ready, 1)

            pool.wait_ge(h1_stored, 16 * NT)
            pool.wait_ge(h1_scaled, NT)
            pool.wait_ge(gidx_ready, 3)
            gather().then_inc(xg_landed, 16)
            pool.wait_ge(most_ready, 2)

            def hidden_of(n):
                pool.wait_ge(acc_stored, 16 * (NT + 1))
                pool.wait_ge(act_step, n)
                pool.wait_ge(sig_ready, n)
                nc.gpsimd.tensor_tensor(up[:], up[:], sig[:], ALU.mult).then_inc(hid_ready, 1)

            def add_rows(e, before, added):
                tokens = tokens_of(e)
                nc.gpsimd.tensor_copy(sidx[:], sidx_all[:, bass.ds(e, 1)]).then_inc(sidx_ready, 1)
                pool.wait_ge(acc_stored, 16 * (NT + 1))
                pool.wait_ge(sidx_ready, before)
                pool.wait_ge(y_ready, before)
                sized(scatter, tokens, rows_added)
                pool.wait_ge(rows_added, added)
                pool.sem_inc(y_free, 1)

            def gather_ahead(e, listed_e1, turned_e):
                tokens = tokens_of(e + 1)
                pool.wait_ge(h1_stored, 16 * NT)
                pool.wait_ge(gidx_ready, listed_e1)
                pool.wait_ge(xg_turned, turned_e)
                sized(gather, tokens, xg_landed)

            gather_ahead(0, 6, 1)
            hidden_of(1)
            gather_ahead(1, 9, 2)
            with pool.Fori(2, E - 1) as e:
                count_e, listed_e1, turned_e, before = \
                    pool.to_reg(e), pool.to_reg(e * 3 + 6), pool.to_reg(e + 1), pool.to_reg(e - 1)
                added = pool.to_reg((e - 1) * 16)
                hidden_of(count_e)
                gather_ahead(e, listed_e1, turned_e)
                add_rows(e - 2, before, added)
            hidden_of(E - 1)
            add_rows(E - 3, E - 2, (E - 2) * 16)
            for e in (E - 2, E - 1):
                add_rows(e, e + 1, (e + 1) * 16)

            pool.wait_ge(most_ready, 2)
            largest = pool.value_load(most[0:1, 0:1], min_val=0, max_val=SEQ)
            with pool.If(largest > P):
                pool.wait_ge(x_tables, 1)
                pool.sem_inc(x_free, 1)
                with pool.Fori(0, NX) as n:
                    need = pool.value_load(over_i[0:1, bass.ds(n, 1)], min_val=0, max_val=1)
                    with pool.If(need > 0):
                        q = pool.value_load(seq_i[0:1, bass.ds(n, 1)], min_val=1, max_val=NX)
                        listed_q = pool.to_reg(q * 3)
                        pool.wait_ge(h1_stored, 16 * NT)
                        pool.wait_ge(x_gidx, listed_q)
                        gather().then_inc(x_rows, 16)
                        pool.wait_ge(acc_stored, 16 * (NT + 1))
                        pool.wait_ge(x_y, q)
                        scatter().then_inc(x_added, 16)
                        pool.wait_ge(x_added, q * 16)
                        pool.sem_inc(x_free, 1)
            pool.sem_inc(x_end, 1)

            pool.wait_ge(wide2_landed, 32)
            for t in range(NT - 1):
                pool.wait_ge(last_scaled, t + 1)
                nc.gpsimd.tensor_tensor(h1[:, t, :], h1[:, t, :], bias2, ALU.add).then_inc(last_ready[t], 1)

        @block.vector
        def _(dve):
            nc.vector.memset(ones16[:], 1.0).then_inc(small_cast, 1)
            nc.vector.memset(place[:], 0.0).then_inc(small_cast, 1)
            nc.vector.memset(value[:], 0.0).then_inc(small_cast, 1)
            dve.wait_ge(masks_landed, 16)
            nc.vector.tensor_copy(tri16[:], msk[:, M_TRI:M_TRI + P]).then_inc(small_cast, 1)
            nc.vector.tensor_copy(three16[:], msk[:, M_ONE3:M_ONE3 + P]).then_inc(small_cast, 1)

            def halo_in(t):
                dve.wait_ge(halo_copied, 1)
                dve.wait_ge(pooled_copied, t + 1)
                first_tokens = turned[:, t % 2, :, 0:HALO]
                nc.vector.tensor_tensor(first_tokens, first_tokens, halo_t[:, :, t * HALO:(t + 1) * HALO], ALU.add)\
                    .then_inc(pooled_whole, 1)

            dve.wait_ge(wide_ready, 1)
            dve.wait_ge(pw_landed, 16)
            pw_v = pw[:].rearrange("p (g k) n -> p g k n", g=NG)
            scale_v = wide[:, 0, :].rearrange("p (g n) -> p g n", g=NG)
            for k in range(2):
                nc.vector.tensor_tensor(pw_v[:, :, k, :], pw_v[:, :, k, :], scale_v, ALU.mult).then_inc(pw_scaled, 1)
            halo_in(0)
            halo_in(1)

            dve.wait_ge(small_cast, 5)
            dve.wait_ge(consts_landed, 16)
            tokens = cst[:, C_TOK:C_TOK + NT].unsqueeze(2).to_broadcast([P, NT, E])
            nc.vector.tensor_copy(value[:, :, :, 0], tokens).then_inc(small_cast, 1)

            dve.wait_ge(biases_landed, 32)
            nc.vector.tensor_copy(bpart[:, 0, :], brow[:]).then_inc(bias_step, 1)
            dve.wait_ge(bias_step, 1)
            nc.vector.tensor_tensor(bres, brow[:], bpart[:, 0, :], ALU.subtract).then_inc(bias_step, 1)
            dve.wait_ge(bias_step, 2)
            nc.vector.tensor_copy(bpart[:, 1, :], bres).then_inc(bias_step, 1)
            dve.wait_ge(bias_step, 3)
            nc.vector.tensor_tensor(brow[:], bres, bpart[:, 1, :], ALU.subtract).then_inc(bias_step, 1)
            dve.wait_ge(bias_step, 4)
            nc.vector.tensor_copy(bpart[:, 2, :], brow[:]).then_inc(bias_step, 1)

            def moments(t, src, step, done):
                for b in range(2):
                    nc.vector.bn_stats(stats[:, t, b, :], src[:, b * BANK:(b + 1) * BANK]).then_inc(step, 1)
                dve.wait_ge(step, 2 * t + 2)
                nc.vector.bn_aggr(mv[:, t, :], stats[:, t, :, :].rearrange("p b n -> p (b n)")).then_inc(done, 1)
                dve.wait_ge(done, t + 1)

            def inverse_root(t, step, n=1):
                r, f, v, done = rstd[:, t:t + n], fix[:, t:t + n], var[:, t:t + n], 4 * (t // n)
                nc.vector.reciprocal(r, std[:, t:t + n]).then_inc(step, 1)
                dve.wait_ge(step, done + 1)
                if n == 1:
                    nc.vector.scalar_tensor_tensor(out=f, in0=r, scalar=v, in1=r, op0=ALU.mult, op1=ALU.mult)\
                        .then_inc(step, 1)
                else:
                    nc.vector.tensor_tensor(f, r, r, ALU.mult).then_inc(step, 1)
                    dve.wait_ge(step, done + 2)
                    nc.vector.tensor_tensor(f, f, v, ALU.mult).then_inc(last_square, 1)
                    dve.wait_ge(last_square, t // n + 1)
                dve.wait_ge(step, done + 2)
                nc.vector.tensor_scalar(f, f, -0.5, 1.5, ALU.mult, ALU.add).then_inc(step, 1)
                dve.wait_ge(step, done + 3)
                nc.vector.tensor_tensor(r, r, f, ALU.mult).then_inc(step, 1)
                dve.wait_ge(step, done + 4)

            def centre(t, src, gain):
                return nc.vector.scalar_tensor_tensor(out=h1[:, t, :], in0=src, scalar=mv[:, t, 0:1], in1=gain,
                                                      op0=ALU.subtract, op1=ALU.mult)

            def spread(t, bias):
                return nc.vector.scalar_tensor_tensor(out=h1[:, t, :], in0=h1[:, t, :], scalar=rstd[:, t:t + 1],
                                                      in1=bias, op0=ALU.mult, op1=ALU.add)

            for t in range(NT):
                dve.wait_ge(mixed, t + 1)
                src = (ps_y if t % 2 == 0 else ps_t)[:].rearrange("p b n -> p (b n)")
                nc.vector.scalar_tensor_tensor(out=z[:, t, :], in0=xin[:, t, :], scalar=ALPHA, in1=src,
                                               op0=ALU.mult, op1=ALU.add).then_inc(mix_evacuated, 1)
                dve.wait_ge(mix_evacuated, t + 1)
                moments(t, z[:, t, :], ln_step, stats_ready)
                nc.vector.tensor_scalar(var[:, t:t + 1], mv[:, t, 1:2], LN_EPS, None, ALU.add).then_inc(var_ready, 1)
                if t == 0:
                    dve.wait_ge(wide_ready, 2)
                centre(t, z[:, t, :], wide[:, 1, :]).then_inc(centred, 1)
                dve.wait_ge(std_ready, t + 1)
                inverse_root(t, rstd_step)
                if t + 2 < NT:
                    halo_in(t + 2)
                if t >= NT // 2:
                    dve.wait_ge(wide_ready, 3)
                    dve.wait_ge(centred, t + 1)
                    if t == NT // 2:
                        dve.wait_ge(h1_ready, NT // 2)
                    spread(t, wide[:, 2, :]).then_inc(h1_ready, 1)

            def low_part(e, unit):
                dve.wait_ge(high_ready, nth(e, unit) + 1)
                s = ring_slot(e, unit)
                nc.vector.tensor_tensor(low[:, s, :], raw(e, unit), high[:, s, :].bitcast(F32), ALU.subtract)\
                    .then_inc(low_ready, 1)

            dve.wait_ge(router_landed, 32)
            experts = cst[:, C_EXP:C_EXP + E].unsqueeze(1).to_broadcast([P, TOPK, E])
            for t in range(NT):
                dve.wait_ge(logits_done, t + 1)
                src = (ps_y if t % 2 == 0 else ps_t)[:, 0, 0:E]
                nc.vector.tensor_tensor(logit[:, t, :], src, rb[:], ALU.add).then_inc(logits_read, 1)
                dve.wait_ge(logits_read, t + 1)
                nc.vector.max(top[:, t, :], logit[:, t, :]).then_inc(route_step, 1)
                dve.wait_ge(route_step, 4 * t + 1)
                nc.vector.max_index(topi[:, t, :], top[:, t, :], logit[:, t, :]).then_inc(route_step, 1)
                nc.vector.tensor_scalar(gexp[:, t, :], logit[:, t, :], top[:, t, 0:1], None, ALU.subtract)\
                    .then_inc(exp_in, 1)
                dve.wait_ge(route_step, 4 * t + 2)
                nc.vector.tensor_copy(topf[:, t, :], topi[:, t, :]).then_inc(route_step, 1)
                dve.wait_ge(route_step, 4 * t + 3)
                nc.vector.tensor_tensor(pick[:, t], topf[:, t, 0:TOPK].unsqueeze(2).to_broadcast([P, TOPK, E]),
                                        experts, ALU.is_equal).then_inc(route_step, 1)
                dve.wait_ge(route_step, 4 * t + 4)
                nc.vector.tensor_reduce(chosen[:, t, :], pick[:, t].rearrange("p k e -> p e k"), AX.X, ALU.add)\
                    .then_inc(chosen_step, 1)
                dve.wait_ge(chosen_step, t + 1)
                nc.vector.tensor_copy(chosen16[:, t, :], chosen[:, t, :]).then_inc(chosen_ready, 1)
            rs = 4 * NT
            dve.wait_ge(exp_done, 1)
            nc.vector.tensor_tensor(gexp[:], gexp[:], chosen[:], ALU.mult).then_inc(route_step, 1)
            dve.wait_ge(route_step, rs + 1)
            nc.vector.tensor_reduce(gsum[:], gexp[:], AX.X, ALU.add).then_inc(route_step, 1)
            dve.wait_ge(route_step, rs + 2)
            nc.vector.reciprocal(gsum[:], gsum[:]).then_inc(route_step, 1)
            dve.wait_ge(route_step, rs + 3)
            dve.wait_ge(small_cast, 6)
            nc.vector.tensor_tensor(value[:, :, :, 1], gexp[:], gsum[:].unsqueeze(2).to_broadcast([P, NT, E]),
                                    ALU.mult).then_inc(place_ready, 1)
            dve.wait_ge(ranked, 1)
            nc.vector.scalar_tensor_tensor(out=place[:],
                                           in0=ps_y[:, 1, 0:NT * E].rearrange("p (t e) -> p t e", t=NT), scalar=1.0,
                                           in1=chosen[:], op0=ALU.add, op1=ALU.mult).then_inc(place_ready, 1)
            dve.wait_ge(place_ready, 2)

            def one_hot(at):
                return nc.vector.tensor_tensor(
                    hot[:], at.to_broadcast([P, NT, P]),
                    cst[:, C_SLOT:C_SLOT + P].unsqueeze(1).to_broadcast([P, NT, P]), ALU.is_equal)

            listed = ps_t[:, 0, 0:2]

            def list_part(e):
                if isinstance(e, int):
                    at, what = place[:, :, e:e + 1], value[:, :, e, :]
                else:
                    at = place[:, :, bass.ds(e, 1)]
                    what = value[:, :, bass.ds(e, 1), :].rearrange("p t o c -> p t (o c)")
                one_hot(at).then_inc(hot_step, 1)
                nc.vector.tensor_copy(val[:], what).then_inc(hot_step, 1)

            def read_list(e):
                if isinstance(e, int):
                    slot_e, sidx_e = slot[:, e, :], sidx_all[:, e:e + 1]
                else:
                    slot_e = slot[:, bass.ds(e, 1), :].rearrange("p o c -> p (o c)")
                    sidx_e = sidx_all[:, bass.ds(e, 1)]
                dve.wait_ge(hot_used, e + 1)
                if not (isinstance(e, int) and e == 0):
                    dve.wait_ge(xg_landed, e * 16)
                nc.vector.tensor_copy(slot_e, listed).then_inc(gidx_ready, 1)
                nc.vector.tensor_scalar(sidx_e, listed[:, 0:1], float(ABSENT), cst[:, C_SPARE:C_SPARE + 1],
                                        ALU.add, ALU.min).then_inc(gidx_ready, 1)
                nc.vector.tensor_scalar(gidx[:], listed[:, 0:1], float(ABSENT), None, ALU.add).then_inc(gidx_ready, 1)

            list_part(0)
            read_list(0)

            nc.vector.tensor_copy(count[:], ps_t[0:1, 1, 0:E]).then_inc(route_step, 1)
            dve.wait_ge(route_step, rs + 4)
            nc.vector.tensor_reduce(most[:], count[:], AX.X, ALU.max).then_inc(most_ready, 1)
            nc.vector.tensor_copy(tally[:], count[:]).then_inc(most_ready, 1)

            def clamp_gate():
                return nc.vector.tensor_scalar(gate[:], ps_gu[:, 0:2, :].rearrange("p b n -> p (b n)"), LIMIT, None,
                                               ALU.min)

            def clamp_up():
                return nc.vector.tensor_scalar(up[:], ps_gu[:, 2:4, :].rearrange("p b n -> p (b n)"), LIMIT, -LIMIT,
                                               ALU.min, ALU.max)

            def up_gate():
                return nc.vector.scalar_tensor_tensor(out=up[:], in0=up[:], scalar=1.0, in1=gate[:],
                                                      op0=ALU.add, op1=ALU.mult)

            def hidden():
                return nc.vector.tensor_tensor(up[:], up[:], sig[:], ALU.mult)

            def low_turned(dst, top_part):
                return nc.vector.tensor_tensor(dst[:].rearrange("p k n -> p (k n)"),
                                               ps_t[:].rearrange("p b n -> p (b n)"),
                                               top_part[:].rearrange("p k n -> p (k n)").bitcast(F32), ALU.subtract)

            def iteration(e):
                first, last = (isinstance(e, int) and e == n for n in (0, E - 1))
                for unit in UNITS:
                    if unit not in done_before(e):
                        low_part(e, unit)
                    if first and unit == (DN, 0):
                        low_part(1, (GU, 0))
                    if unit == (GU, 0) and not last:
                        list_part(e + 1)
                    if unit == (GU, 1) and not first:
                        finish_gate(e)
                    if unit == (GU, 3) and not last:
                        read_list(e + 1)
                    if unit == (DN, 0) and not first:
                        dve.wait_ge(ht_high_ready, e)
                        low_turned(ht_low, ht_high).then_inc(ht_low_ready, 1)
                    if unit == (DN, 1):
                        if first:
                            dve.wait_ge(acc_stored, 16 * (NT + 1))
                        dve.wait_ge(split_used, nth(e, (GU, KD - 1)) + 1)
                        clamp_gate().then_inc(gate_ready, 1)
                    if unit == ((DN, 1) if last else (DN, 2)):
                        clamp_up().then_inc(up_ready, 1)
                    if unit == (DN, 3) and not last:
                        dve.wait_ge(xt_high_ready, e + 2)
                        low_turned(xt_low, xt_high).then_inc(xt_low_ready, 1)
                        if first:
                            low_part(1, (GU, 1))
                    if unit == (DN, 2) and last:
                        finish_gate(E)
                        dve.wait_ge(act_step, E)
                        dve.wait_ge(sig_ready, E)
                        hidden().then_inc(hid_ready, 1)

            def finish_gate(n):
                dve.wait_ge(gate_ready, n)
                dve.wait_ge(up_ready, n)
                up_gate().then_inc(act_step, 1)

            for k in range(RING):
                low_part(0, (GU, k))
            dve.wait_ge(xt_high_ready, 1)
            low_turned(xt_low, xt_high).then_inc(xt_low_ready, 1)
            iteration(0)
            iteration(1)
            with dve.Fori(2, E - 1) as e:
                iteration(e)
            iteration(E - 1)
            for unit in UNITS[KD:]:
                low_part(E, unit)
                if unit == (DN, 0):
                    dve.wait_ge(ht_high_ready, E)
                    low_turned(xt_low, xt_high).then_inc(ht_low_ready, 1)

            dve.wait_ge(most_ready, 2)
            largest = dve.value_load(most[0:1, 0:1], min_val=0, max_val=SEQ)
            with dve.If(largest > P):
                for j in range(MORE):
                    nc.vector.tensor_scalar(over[:, j * E:(j + 1) * E], count[:], float(P * (j + 1)), None, ALU.is_gt)\
                        .then_inc(x_step, 1)
                    nc.vector.tensor_scalar(place_x[:, :, j * E:(j + 1) * E], place[:], float(-P * (j + 1)),
                                            None, ALU.add).then_inc(x_step, 1)
                dve.wait_ge(x_step, 2 * MORE)
                nc.vector.tensor_tensor_scan(seq_f[:], over[:], over[:], 0.0, ALU.add, ALU.max).then_inc(x_step, 1)
                nc.vector.tensor_copy(over_i[:], over[:]).then_inc(x_step, 1)
                dve.wait_ge(x_step, 2 * MORE + 2)
                nc.vector.tensor_copy(seq_i[:], seq_f[:]).then_inc(x_tables, 1)
                dve.wait_ge(x_tables, 1)
                for j in range(MORE):
                    with dve.Fori(0, E) as e:
                        need = dve.value_load(over_i[0:1, bass.ds(e + j * E, 1)], min_val=0, max_val=1)
                        with dve.If(need > 0):
                            q = dve.value_load(seq_i[0:1, bass.ds(e + j * E, 1)], min_val=1, max_val=NX)
                            dve.wait_ge(x_free, q)
                            one_hot(place_x[:, :, bass.ds(e + j * E, 1)]).then_inc(x_hot, 1)
                            nc.vector.tensor_copy(
                                val[:], value[:, :, bass.ds(e, 1), :].rearrange("p t o c -> p t (o c)"))\
                                .then_inc(x_hot, 1)
                            dve.wait_ge(x_listed, q)
                            nc.vector.tensor_copy(slot_x[:], listed).then_inc(x_gidx, 1)
                            nc.vector.tensor_scalar(sidx[:], listed[:, 0:1], float(ABSENT),
                                                    cst[:, C_SPARE:C_SPARE + 1], ALU.add, ALU.min).then_inc(x_gidx, 1)
                            nc.vector.tensor_scalar(gidx[:], listed[:, 0:1], float(ABSENT), None, ALU.add)\
                                .then_inc(x_gidx, 1)
                            dve.wait_ge(x_gu, q)
                            clamp_gate().then_inc(x_gate, 1)
                            clamp_up().then_inc(x_up, 1)
                            dve.wait_ge(x_gate, q)
                            dve.wait_ge(x_up, q)
                            up_gate().then_inc(x_upgate, 1)
                            dve.wait_ge(x_upgate, q)
                            dve.wait_ge(x_sig, q)
                            hidden().then_inc(x_hid, 1)

            for t in range(0, NT, 2):
                for u in (t, t + 1):
                    dve.wait_ge(sums_landed[u], 16)
                    moments(u, xin[:, u, :], last_step, last_stats)
                nc.vector.tensor_scalar(var[:, t:t + 2], mv[:, t:t + 2, 1], LN_EPS, None, ALU.add).then_inc(last_var, 1)
                if t == 0:
                    dve.wait_ge(wide2_landed, 32)
                centre(t, xin[:, t, :], gain2).then_inc(last_centred, 1)
                dve.wait_ge(last_std, t // 2 + 1)
                inverse_root(t, last_rstd, 2)
                centre(t + 1, xin[:, t + 1, :], gain2).then_inc(last_centred, 1)
            dve.wait_ge(last_centred, NT)
            spread(NT - 1, bias2).then_inc(last_ready[NT - 1], 1)

        @block.tensor
        def _(pe):
            def warm(times):
                for _ in range(times):
                    nc.tensor.matmul(ps_gu[:, 3, :], ones16[:], d_bias[:, 0:BANK], start=True, stop=True)

            pe.wait_ge(zeros_set, 1)
            pe.wait_ge(small_cast, 1)
            warm(WARM)

            pe.wait_ge(masks_landed, 16)
            pe.wait_ge(halo_landed, 16 * NT)
            for c in range(KD):
                at = M_BEFORE + (c // 2) * NT * HALO
                last = nc.tensor.matmul(ps_t[:, 0, c * NT * HALO:(c + 1) * NT * HALO], halo[:, c * P:(c + 1) * P],
                                        msk[0:NT * HALO, at:at + NT * HALO], start=True, stop=True)
            last.then_inc(halo_pooled, 1)

            def pool_rows(t):
                pe.wait_ge(x_landed[t], 16)
                if t >= 2:
                    pe.wait_ge(pooled_copied, t - 1)
                for c in range(KD):
                    dst = ps_gu[:, 2 * (t % 2) + c // 4, (c % 4) * P:(c % 4 + 1) * P]
                    own = M_OWN + (c // 2) * P
                    last = nc.tensor.matmul(dst, xin[:, t, c * P:(c + 1) * P], msk[:, own:own + P],
                                            start=True, stop=True)
                last.then_inc(pooled, 1)

            def mix_rows(t):
                pe.wait_ge(pooled_whole, t + 1)
                pe.wait_ge(pw_scaled, 2)
                if t >= 2:
                    pe.wait_ge(mix_evacuated, t - 1)
                dst = (ps_y if t % 2 == 0 else ps_t)[:].rearrange("p b n -> p (b n)")
                for g in range(NG):
                    for k in range(2):
                        last = nc.tensor.matmul(dst[:, g * GW:(g + 1) * GW], turned[:, t % 2, 2 * g + k, :],
                                                pw[:, 2 * g + k, :], start=(k == 0), stop=(k == 1))
                last.then_inc(mixed, 1)

            def spread_row(v):
                dst = ps_y if v == 0 else ps_t
                for n in range(2):
                    last = nc.tensor.matmul(dst[:, n, :], msk[0:1, M_ONE3:M_ONE3 + P],
                                            wide[0:1, v, n * BANK:(n + 1) * BANK], start=True, stop=True)
                last.then_inc(spread_done, 1)

            pe.wait_ge(scale_landed, 16)
            spread_row(0)
            pool_rows(0)
            pool_rows(1)
            pe.wait_ge(wide_landed, 32)
            pe.wait_ge(halo_copied, 1)
            spread_row(1)
            pe.wait_ge(wide_ready, 1)
            mix_rows(0)
            pe.wait_ge(wide_ready, 2)
            spread_row(2)
            pool_rows(2)
            pe.wait_ge(wide_ready, 3)
            mix_rows(1)
            pool_rows(3)
            mix_rows(2)
            mix_rows(3)

            pe.wait_ge(router_landed, 32)
            pe.wait_ge(consts_landed, 16)

            def turn_rows(t):
                pe.wait_ge(h1_ready, t + 1)
                pe.wait_ge(pooled_copied, NT)
                if t >= 2:
                    pe.wait_ge(h1_copied, t - 1)
                turn(ps_gu[:, 2 * (t % 2):2 * (t % 2) + 2, :], h1[:, t, :]).then_inc(h1_turned, 1)

            def route_rows(t):
                pe.wait_ge(h1_copied, t + 1)
                pe.wait_ge(mix_evacuated, NT)
                if t >= 2:
                    pe.wait_ge(logits_read, t - 1)
                dst = (ps_y if t % 2 == 0 else ps_t)[:, 0, 0:E]
                for k in range(KD):
                    last = nc.tensor.matmul(dst, turned[:, t % 2, k, :], rwt[:, k, :], start=(k == 0),
                                            stop=(k == KD - 1))
                last.then_inc(logits_done, 1)

            turn_rows(0)
            turn_rows(1)
            route_rows(0)
            turn_rows(2)
            route_rows(1)
            turn_rows(3)
            route_rows(2)
            route_rows(3)

            pe.wait_ge(chosen_ready, NT)
            pe.wait_ge(small_cast, 6)
            rank = ps_y[:, 1, 0:NT * E]
            for t in range(NT):
                dst = rank[:, t * E:(t + 1) * E]
                for s in range(t):
                    nc.tensor.matmul(dst, ones16[:], chosen16[:, s, :], start=(s == 0), stop=False)
                nc.tensor.matmul(dst, tri16[:], chosen16[:, t, :], start=(t == 0), stop=True)
            for t in range(NT):
                last = nc.tensor.matmul(ps_t[:, 1, 0:E], ones16[:], chosen16[:, t, :], start=(t == 0),
                                        stop=(t == NT - 1))
            last.then_inc(ranked, 1)

            listed = ps_t[:, 0, 0:2]
            pe.wait_ge(hot_step, 2)
            pe.wait_ge(logits_read, NT)
            list_slots(listed).then_inc(hot_used, 1)
            pe.wait_ge(db_landed, 16)
            warm(WARM_AGAIN)
            pe.wait_ge(xg_landed, 16)
            pe.wait_ge(most_ready, 2)
            turn(ps_t, xg[:]).then_inc(xg_turned, 1)

            def gate_up_unit(e, k):
                pe.wait_ge(low_ready, nth(e, (GU, k)) + 1)
                gate_up_parts(k, ring_slot(e, (GU, k))).then_inc(split_used, 1)

            def down_unit(e, j, dst=ps_y):
                pe.wait_ge(low_ready, nth(e, (DN, j)) + 1)
                own = isinstance(e, int) and e == E
                down_parts(j, ring_slot(e, (DN, j)), dst, *((xt_high, xt_low) if own else (ht_high, ht_low)))\
                    .then_inc(split_used, 1)

            def iteration(e):
                first, last = (isinstance(e, int) and e == n for n in (0, E - 1))
                pe.wait_ge(gub_landed, e * 16 + 16)
                if not first:
                    pe.wait_ge(up_ready, e)
                    pe.wait_ge(gate_ready, e)
                gate_up_bias().then_inc(gub_used, 1)
                pe.wait_ge(xt_low_ready, e + 1)
                for k in range(KD):
                    gate_up_unit(e, k)
                    if k == 1 and not last:
                        pe.wait_ge(hot_step, e * 2 + 4)
                        list_slots(listed).then_inc(hot_used, 1)
                    if k == 5 and not first:
                        pe.wait_ge(hid_ready, e)
                        if not last:
                            pe.wait_ge(gidx_ready, e * 3 + 6)
                        turn(ps_t, up[:]).then_inc(hid_turned, 1)
                if not first:
                    pe.wait_ge(ht_low_ready, e)
                if not first:
                    pe.wait_ge(db_landed, e * 16)
                    if not (isinstance(e, int) and e == 1):
                        pe.wait_ge(y_ready, e - 1)
                    down_bias().then_inc(db_used, 1)
                for j in range(KD // 2):
                    if not first:
                        down_unit(e, j)
                    if j == 1 and not last:
                        pe.wait_ge(xg_landed, e * 16 + 32)
                        turn(ps_t, xg[:]).then_inc(xg_turned, 1)
                    if j == 2 and last:
                        pe.wait_ge(hid_ready, E)
                        turn(ps_t, up[:]).then_inc(hid_turned, 1)

            iteration(0)
            iteration(1)
            with pe.Fori(2, E - 1) as e:
                iteration(e)
            iteration(E - 1)
            pe.wait_ge(gate_ready, E)
            pe.wait_ge(up_ready, E)
            pe.wait_ge(db_landed, E * 16)
            down_bias(ps_gu)
            pe.wait_ge(ht_low_ready, E)
            for j in range(KD // 2):
                down_unit(E, j, ps_gu)

            largest = pe.value_load(most[0:1, 0:1], min_val=0, max_val=SEQ)
            with pe.If(largest > P):
                pe.wait_ge(x_tables, 1)
                with pe.Fori(0, NX) as n:
                    need = pe.value_load(over_i[0:1, bass.ds(n, 1)], min_val=0, max_val=1)
                    with pe.If(need > 0):
                        q = pe.value_load(seq_i[0:1, bass.ds(n, 1)], min_val=1, max_val=NX)
                        pe.wait_ge(x_hot, q * 2)
                        list_slots(listed).then_inc(x_listed, 1)
                        pe.wait_ge(x_rows, q * 16)
                        turn(ps_t, xg[:]).then_inc(x_turned, 1)
                        pe.wait_ge(x_weights, q * (16 * (KD + 3)))
                        pe.wait_ge(x_xt, q)
                        gate_up_bias()
                        for k in range(KD):
                            last = gate_up(k)
                        last.then_inc(x_gu, 1)
                        pe.wait_ge(x_hid, q)
                        turn(ps_t, up).then_inc(x_hturned, 1)
                        pe.wait_ge(x_ht, q)
                        down_bias()
                        for k in range(KD):
                            last = down(k)
                        last.then_inc(x_d, 1)


_INS = ["x", "meta_tokens", "consts", "masks", "pool_w", "pool_scale", "router_wt", "router_b", "moe_wgu", "moe_bgu",
        "moe_wd", "moe_bd", "ln_g", "ln_b"]


def kernel(**inputs):
    import concourse.bacc as bacc
    from concourse.bass_utils import run_bass_kernel_spmd

    given = {n: np.ascontiguousarray(a) for n, a in inputs.items()}
    given["consts"], given["masks"] = shape_constants()
    given["router_wt"] = np.ascontiguousarray(given["router_w"][0].T)
    given["moe_wgu"] = given["moe_wgu"][0]
    given["moe_wd"] = given["moe_wd"][0]
    nc = bacc.Bacc("TRN2", target_bir_lowering=False, num_devices=1)
    arrays, args = {}, []
    for name in _INS:
        a = given[name]
        arrays[f"in_{name}"] = a
        args.append(nc.dram_tensor(f"in_{name}", a.shape, mybir.dt.from_np(a.dtype), kind="ExternalInput").ap())
    out = nc.dram_tensor("out_rows", (1, SEQ, D), F32, kind="ExternalOutput").ap()
    trunk(nc, *args, out)
    return run_bass_kernel_spmd(nc, [arrays], core_ids=[0]).results[0]["out_rows"]
```
